# Optimizing a Trainium2 kernel written in Bass

```python
import jax, jax.numpy as jnp
from jax import lax
import numpy as np

D_MODEL = 1024
BATCH = 1
SEQ = 512
DEPTH = 1

N_META = 16
POOL_WIDTH = D_MODEL // 2
POOL_WINDOWS = (2, 4, 8, 16)
POOL_GROUP = POOL_WIDTH // len(POOL_WINDOWS)
N_HEADS = 8
HEAD_DIM = 64
ATTN_WIDTH = N_HEADS * HEAD_DIM
Q_BLOCK = 128
RMS_EPS = 1e-6
IN_SIZES = (POOL_WIDTH, POOL_WIDTH, ATTN_WIDTH, ATTN_WIDTH, ATTN_WIDTH, ATTN_WIDTH, N_HEADS, D_MODEL, D_MODEL)
N_IN = 2 * POOL_WIDTH + 4 * ATTN_WIDTH + N_HEADS + 2 * D_MODEL


def _split_points():
    pts, acc = [], 0
    for s in IN_SIZES[:-1]:
        acc += s
        pts.append(acc)
    return pts

def rmsnorm(x, g):
    xf = x.astype(jnp.float32)
    xf = xf * lax.rsqrt(jnp.mean(xf * xf, axis=-1, keepdims=True) + RMS_EPS)
    return (xf * g.astype(jnp.float32)).astype(x.dtype)

def causal_multiscale_pool(u, pool_w, pool_scale):
    B, L, _ = u.shape
    groups = jnp.split(u, len(POOL_WINDOWS), axis=-1)
    pos = jnp.arange(L, dtype=jnp.float32)[:, None]
    pooled = []
    for w, ug in zip(POOL_WINDOWS, groups):
        uf = ug.astype(jnp.float32)
        c = jnp.cumsum(uf, axis=1)
        c_prev = jnp.pad(c, ((0, 0), (w, 0), (0, 0)))[:, :L]
        count = jnp.minimum(pos + 1.0, float(w))
        pooled.append((c - c_prev) / count - uf)
    p = jnp.stack(pooled, axis=2).astype(u.dtype)
    y = jnp.einsum('blgc,gcd->blgd', p, pool_w)
    return y.reshape(B, L, POOL_WIDTH) * pool_scale

def forgetting_attention(q, k, v, log_f):
    B, L, H, Dh = q.shape
    pad = (Q_BLOCK - L % Q_BLOCK) % Q_BLOCK
    padw = ((0, 0), (pad, 0), (0, 0), (0, 0))
    qp, kp, vp = jnp.pad(q, padw), jnp.pad(k, padw), jnp.pad(v, padw)
    c = jnp.cumsum(log_f, axis=1)
    c = jnp.transpose(jnp.pad(c, ((0, 0), (pad, 0), (0, 0))), (0, 2, 1))
    Lp = L + pad
    scale = 1.0 / np.sqrt(HEAD_DIM)
    outs = []
    for i in range(Lp // Q_BLOCK):
        q0, q1 = i * Q_BLOCK, (i + 1) * Q_BLOCK
        qb, kb, vb = qp[:, q0:q1], kp[:, :q1], vp[:, :q1]
        s = jnp.einsum('bqhd,bkhd->bhqk', qb, kb).astype(jnp.float32) * scale
        s = s + c[:, :, q0:q1, None] - c[:, :, None, :q1]
        q_idx = jnp.arange(q0, q1)[:, None]
        k_idx = jnp.arange(q1)[None, :]
        valid = (k_idx <= q_idx) & ((k_idx >= pad) | (k_idx == q_idx))
        s = jnp.where(valid, s, -jnp.inf)
        p = jax.nn.softmax(s, axis=-1)
        outs.append(jnp.einsum('bhqk,bkhd->bqhd', p.astype(vb.dtype), vb))
    o = jnp.concatenate(outs, axis=1)[:, pad:]
    return o

def hybrid_layer(x, norm_g, w_in, b_forget, pool_w, pool_scale, w_up_pool, w_up_attn, w_out):
    B, L, _ = x.shape
    h = rmsnorm(x, norm_g)
    proj = jnp.einsum('bld,dn->bln', h, w_in)
    u_pool, z_pool, q, k, v, z_attn, f_logit, g_pool, g_attn = jnp.split(proj, _split_points(), axis=-1)
    y_pool = causal_multiscale_pool(u_pool, pool_w, pool_scale) * jax.nn.silu(z_pool)
    q = q.reshape(B, L, N_HEADS, HEAD_DIM)
    k = k.reshape(B, L, N_HEADS, HEAD_DIM)
    v = v.reshape(B, L, N_HEADS, HEAD_DIM)
    log_f = jax.nn.log_sigmoid((f_logit + b_forget).astype(jnp.float32))
    y_attn = forgetting_attention(q, k, v, log_f).reshape(B, L, ATTN_WIDTH) * jax.nn.silu(z_attn)
    merged = (jax.nn.sigmoid(g_pool) * jnp.einsum('blc,cd->bld', y_pool, w_up_pool)
              + jax.nn.sigmoid(g_attn) * jnp.einsum('blc,cd->bld', y_attn, w_up_attn))
    return x + jnp.einsum('bld,de->ble', merged, w_out)

def first_inputs(seed: int = 0) -> dict:
    key = jax.random.key(seed)
    ks = jax.random.split(key, 12)
    f0 = sum(IN_SIZES[:6])
    x = jax.random.normal(ks[0], (BATCH, SEQ, D_MODEL), jnp.float32)
    meta_tokens = jax.random.normal(ks[1], (N_META, D_MODEL), jnp.float32)
    norm_g = 1.0 + 0.02 * jax.random.normal(ks[2], (DEPTH, D_MODEL), jnp.float32)
    w_in = jax.random.normal(ks[3], (DEPTH, D_MODEL, N_IN), jnp.float32) * D_MODEL ** -0.5
    w_in = w_in.at[:, :, f0:f0 + N_HEADS].multiply(0.1)
    b_forget = (jnp.linspace(1.0, 6.0, N_HEADS, dtype=jnp.float32)[None, :]
                + 0.1 * jax.random.normal(ks[4], (DEPTH, N_HEADS), jnp.float32))
    pool_w = jax.random.normal(ks[5], (DEPTH, len(POOL_WINDOWS), POOL_GROUP, POOL_GROUP), jnp.float32) * POOL_GROUP ** -0.5
    pool_scale = 1.0 + 0.1 * jax.random.normal(ks[6], (DEPTH, POOL_WIDTH), jnp.float32)
    w_up_pool = jax.random.normal(ks[7], (DEPTH, POOL_WIDTH, D_MODEL), jnp.float32) * POOL_WIDTH ** -0.5
    w_up_attn = jax.random.normal(ks[8], (DEPTH, ATTN_WIDTH, D_MODEL), jnp.float32) * ATTN_WIDTH ** -0.5
    w_out = jax.random.normal(ks[9], (DEPTH, D_MODEL, D_MODEL), jnp.float32) * D_MODEL ** -0.5
    final_norm_g = 1.0 + 0.02 * jax.random.normal(ks[10], (D_MODEL,), jnp.float32)
    return {"x": x, "meta_tokens": meta_tokens, "norm_g": norm_g, "w_in": w_in,
            "b_forget": b_forget, "pool_w": pool_w, "pool_scale": pool_scale,
            "w_up_pool": w_up_pool, "w_up_attn": w_up_attn, "w_out": w_out,
            "final_norm_g": final_norm_g}

def first_block(x, meta_tokens, norm_g, w_in, b_forget, pool_w, pool_scale, w_up_pool, w_up_attn, w_out, final_norm_g):
    B = x.shape[0]
    meta = jnp.broadcast_to(meta_tokens.astype(x.dtype)[None], (B, N_META, D_MODEL))
    h = jnp.concatenate([meta, x], axis=1)
    for l in range(DEPTH):
        h = hybrid_layer(h, norm_g[l], w_in[l], b_forget[l], pool_w[l], pool_scale[l],
                         w_up_pool[l], w_up_attn[l], w_out[l])
    h = rmsnorm(h, final_norm_g)
    return h[:, N_META:]


N_HEADS_2 = D_MODEL // HEAD_DIM
N_SB_HEADS = N_HEADS_2 // 2
N_CA_HEADS = N_HEADS_2 - N_SB_HEADS
D_SB = N_SB_HEADS * HEAD_DIM
D_CA = N_CA_HEADS * HEAD_DIM
D_IN = 3 * D_SB + 3 * D_CA
D_FF = 4 * D_MODEL
CHUNK = 64
LEFT_CHUNKS = 8
BAND = (LEFT_CHUNKS + 1) * CHUNK
REL_CLIP = 128
N_REL = 2 * REL_CLIP + 1
EPS = 1e-6
NEG_INF = -1e30


def rmsnorm_2(x, g):
    xf = x.astype(jnp.float32)
    y = xf * lax.rsqrt(jnp.mean(xf * xf, axis=-1, keepdims=True) + EPS)
    return (y * g.astype(jnp.float32)).astype(x.dtype)

def stick_breaking_attention(q, k, v):
    B, S, H, d = q.shape
    scale = d ** -0.5
    outs = []
    for start in range(0, S, Q_BLOCK):
        end = start + Q_BLOCK
        qb = q[:, start:end]
        kb = k[:, :end]
        vb = v[:, :end]
        z = jnp.einsum('bqhd,bkhd->bhqk', qb, kb).astype(jnp.float32) * scale
        t_idx = start + jnp.arange(Q_BLOCK)[:, None]
        s_idx = jnp.arange(end)[None, :]
        strict = s_idx < t_idx
        log_beta = jax.nn.log_sigmoid(z)
        log_1m_beta = jnp.where(strict, jax.nn.log_sigmoid(-z), 0.0)
        suffix = lax.cumsum(log_1m_beta, axis=3, reverse=True) - log_1m_beta
        w = jnp.where(strict, jnp.exp(log_beta + suffix), 0.0)
        outs.append(jnp.einsum('bhqk,bkhd->bqhd', w.astype(v.dtype), vb))
    return jnp.concatenate(outs, axis=1)

def chunked_relpos_attention(q, k, v, rel_bias):
    B, S, H, d = q.shape
    nc = S // CHUNK
    pad = LEFT_CHUNKS * CHUNK
    kp = jnp.pad(k, ((0, 0), (pad, 0), (0, 0), (0, 0))).reshape(B, nc + LEFT_CHUNKS, CHUNK, H, d)
    vp = jnp.pad(v, ((0, 0), (pad, 0), (0, 0), (0, 0))).reshape(B, nc + LEFT_CHUNKS, CHUNK, H, d)
    k_band = jnp.concatenate([kp[:, i:i + nc] for i in range(LEFT_CHUNKS + 1)], axis=2)
    v_band = jnp.concatenate([vp[:, i:i + nc] for i in range(LEFT_CHUNKS + 1)], axis=2)
    qc = q.reshape(B, nc, CHUNK, H, d)
    s = jnp.einsum('bnqhd,bnkhd->bnhqk', qc, k_band).astype(jnp.float32) * (d ** -0.5)
    qi = jnp.arange(CHUNK)[:, None]
    kj = jnp.arange(BAND)[None, :]
    rel = qi + pad - kj
    rel_idx = jnp.clip(rel, -REL_CLIP, REL_CLIP) + REL_CLIP
    bias = rel_bias[:, rel_idx].astype(jnp.float32)
    s = s + bias[None, None]
    key_pos = jnp.arange(nc)[:, None] * CHUNK + kj - pad
    valid = key_pos >= 0
    s = jnp.where(valid[None, :, None, None, :], s, NEG_INF)
    p = jax.nn.softmax(s, axis=-1)
    out = jnp.einsum('bnhqk,bnkhd->bnqhd', p.astype(v.dtype), v_band)
    return out.reshape(B, S, H, d)

def second_inputs(seed: int = 0) -> dict:
    key = jax.random.key(seed)
    ks = jax.random.split(key, 16)
    f32 = jnp.float32
    x = jax.random.normal(ks[0], (BATCH, SEQ, D_MODEL), f32)
    c = jax.random.normal(ks[1], (BATCH, D_MODEL), f32)
    g_norm1 = 1.0 + 0.01 * jax.random.normal(ks[2], (DEPTH, D_MODEL), f32)
    w_in = jax.random.normal(ks[3], (DEPTH, D_MODEL, D_IN), f32) * D_MODEL ** -0.5
    g_q = 1.0 + 0.01 * jax.random.normal(ks[4], (DEPTH, HEAD_DIM), f32)
    g_k = 1.0 + 0.01 * jax.random.normal(ks[5], (DEPTH, HEAD_DIM), f32)
    rel_bias = 0.1 * jax.random.normal(ks[6], (DEPTH, N_CA_HEADS, N_REL), f32)
    w_o = jax.random.normal(ks[7], (DEPTH, D_MODEL, D_MODEL), f32) * D_MODEL ** -0.5
    g_norm2 = 1.0 + 0.01 * jax.random.normal(ks[8], (DEPTH, D_MODEL), f32)
    w1 = jax.random.normal(ks[9], (DEPTH, D_MODEL, D_FF), f32) * D_MODEL ** -0.5
    w2 = jax.random.normal(ks[10], (DEPTH, D_FF, D_MODEL), f32) * D_FF ** -0.5
    w_ada = jax.random.normal(ks[11], (DEPTH, D_MODEL, 6 * D_MODEL), f32) * (0.5 * D_MODEL ** -0.5)
    b_ada = 0.01 * jax.random.normal(ks[12], (DEPTH, 6 * D_MODEL), f32)
    return {"x": x, "c": c, "g_norm1": g_norm1, "w_in": w_in, "g_q": g_q, "g_k": g_k,
            "rel_bias": rel_bias, "w_o": w_o, "g_norm2": g_norm2, "w1": w1, "w2": w2,
            "w_ada": w_ada, "b_ada": b_ada}

def second_block(x, c, g_norm1, w_in, g_q, g_k, rel_bias, w_o, g_norm2, w1, w2, w_ada, b_ada):
    B, S, D = x.shape
    split_pts = [D_SB, 2 * D_SB, 3 * D_SB, 3 * D_SB + D_CA, 3 * D_SB + 2 * D_CA]
    c_act = jax.nn.silu(c)
    for l in range(DEPTH):
        mod = c_act @ w_ada[l] + b_ada[l]
        sh1, sc1, gt1, sh2, sc2, gt2 = [m[:, None, :] for m in jnp.split(mod, 6, axis=-1)]
        h = rmsnorm_2(x, g_norm1[l]) * (1.0 + sc1) + sh1
        proj = h @ w_in[l]
        q_sb, k_sb, v_sb, q_ca, k_ca, v_ca = jnp.split(proj, split_pts, axis=-1)
        hs = lambda t, n: t.reshape(B, S, n, HEAD_DIM)
        o_sb = stick_breaking_attention(hs(q_sb, N_SB_HEADS), hs(k_sb, N_SB_HEADS), hs(v_sb, N_SB_HEADS))
        q_ca = rmsnorm_2(hs(q_ca, N_CA_HEADS), g_q[l])
        k_ca = rmsnorm_2(hs(k_ca, N_CA_HEADS), g_k[l])
        o_ca = chunked_relpos_attention(q_ca, k_ca, hs(v_ca, N_CA_HEADS), rel_bias[l])
        mixed = jnp.concatenate([o_sb.reshape(B, S, D_SB), o_ca.reshape(B, S, D_CA)], axis=-1)
        x = x + gt1 * (mixed @ w_o[l])
        h = rmsnorm_2(x, g_norm2[l]) * (1.0 + sc2) + sh2
        x = x + gt2 * (jnp.square(jax.nn.relu(h @ w1[l])) @ w2[l])
    return x


def setup_inputs(seed=0):
    out = dict(first_inputs(seed))
    for name, value in second_inputs(seed + 1).items():
        if name != "x":
            out[name + "_2"] = value
    return out


def reference(
    x, meta_tokens, norm_g, w_in, b_forget, pool_w, pool_scale, w_up_pool, w_up_attn, w_out,
    final_norm_g, c_2, g_norm1_2, w_in_2, g_q_2, g_k_2, rel_bias_2, w_o_2, g_norm2_2, w1_2,
    w2_2, w_ada_2, b_ada_2,
):
    x = first_block(
        x, meta_tokens, norm_g, w_in, b_forget, pool_w, pool_scale, w_up_pool, w_up_attn, w_out,
        final_norm_g,
    )
    return second_block(
        x, c_2, g_norm1_2, w_in_2, g_q_2, g_k_2, rel_bias_2, w_o_2, g_norm2_2, w1_2, w2_2,
        w_ada_2, b_ada_2,
    )


_drawn_inputs = setup_inputs


def setup_inputs(seed=0):
    import zlib

    import numpy as np

    out = dict(_drawn_inputs(seed))
    spreads = {}
    factors = {'meta_tokens': 3.465,
     'norm_g': 6.23,
     'final_norm_g': 2.872,
     'g_norm1_2': 8.0,
     'g_q_2': 8.0,
     'g_k_2': 8.0,
     'rel_bias_2': 8.0,
     'g_norm2_2': 8.0,
     'b_ada_2': 3.408}
    for name, (base, spread) in spreads.items():
        noise = np.random.default_rng([zlib.crc32(name.encode()), seed]).standard_normal(out[name].shape)
        drawn = base * np.exp(spread * noise) if base else spread * noise
        out[name] = __import__('jax').numpy.asarray(drawn.astype(out[name].dtype))
    for name, factor in factors.items():
        out[name] = (out[name] * factor).astype(out[name].dtype)
    return out
```

```python
from contextlib import ExitStack

import concourse.bass as bass
from concourse import mybir

F32 = mybir.dt.float32
F32R = mybir.dt.float32r
ALU = mybir.AluOpType
ACT = mybir.ActivationFunctionType
AX = mybir.AxisListType

D = 1024
SEQ = 512
META = 16
TOK = META + SEQ
UNIT = 2048
NEG = -1.0e30
EPS = 1e-6

C_U, C_ZP, C_Q, C_K, C_V, C_ZA, C_F, C_GP, C_GA = 0, 512, 1024, 1536, 2048, 2560, 3072, 3080, 4104


def plan():
    ada = [("ada", "w_ada_2", kt, g) for g in range(3) for kt in range(8)]
    out = [("rows", "w_in", kh, C_V) for kh in range(2)]
    out += [("cols", "w_in", C_ZA + 256 * j, C_ZA + 256 * j + 128) for j in range(2)]
    for p in range(4):
        out.append(("cols", "w_in", C_Q + 128 * p, C_K + 128 * p))
        out.append(("cols", "w_in", C_U + 128 * p, C_ZP + 128 * p))
    for e in range(4):
        n = (1, 2, 2) if e == 3 else (2, 1, 2)
        for i, d in enumerate((2 * e, 2 * e + 1)):
            out.append(("cols", "w_in", C_GP + 128 * d, C_GA + 128 * d))
            out += [ada.pop(0) for _ in range(n[i])]
        out.append(("up", "", e, 0))
        out += [ada.pop(0) for _ in range(n[2])]
    for ch in range(2):
        for kh in range(2):
            out.append(("rows", "w_out", kh, 512 * ch))
            out.append(ada.pop(0))
    out += [("rows", "w_in_2", kh, 2560) for kh in range(2)]
    for p in range(4):
        out.append(("cols", "w_in_2", 1536 + 128 * p, 2048 + 128 * p))
    out += [("rows", "w_in_2", kh, 1024) for kh in range(2)]
    for p in range(4):
        out.append(("cols", "w_in_2", 128 * p, 512 + 128 * p))
    for ch in range(2):
        for kh in range(2):
            out.append(("rows", "w_o_2", kh, 512 * ch))
    for q in range(4):
        for j in range(4):
            out.append(("cols", "w1_2", 1024 * q + 256 * j, 1024 * q + 256 * j + 128))
        for ch in range(2):
            for kh in range(2):
                out.append(("rows", "w2_2", 2 * q + kh, 512 * ch))
    assert not ada
    return out


class Sig:

    def __init__(self, sem, step):
        self.sem, self.step, self.n = sem, step, 0

    def now(self):
        return (self, self.n)


class Lane:

    def __init__(self):
        self.ops, self.seen = [], {}

    def __call__(self, method, *args, w=(), s=None, **kw):
        need = {}
        stack = [w]
        while stack:
            one = stack.pop()
            if one is None:
                continue
            if isinstance(one, tuple) and len(one) == 2 and isinstance(one[0], Sig):
                if self.seen.get(one[0], 0) < one[1]:
                    self.seen[one[0]] = need[one[0]] = one[1]
            else:
                stack.extend(one)
        self.ops.append((list(need.items()), method, args, kw, s))
        if s is None:
            return None
        s.n += s.step
        return s.now()

    def run(self, eng):
        for need, method, args, kw, s in self.ops:
            for sig, v in need:
                eng.wait_ge(sig.sem, v)
            ins = method(*args, **kw)
            if s is not None:
                ins.then_inc(s.sem, s.step)


class Bank:

    def __init__(self, ap):
        self.ap, self.free = ap, []


class Ring:
    def __init__(self, banks):
        self.banks, self.n = banks, 0

    def next(self):
        self.n += 1
        return self.banks[(self.n - 1) % len(self.banks)]


def program(nc, x, meta, wall, wf, bf, poolw, pscale, ng, fng, cvec, bada, gn1, gn2, gqk, rel, out):
    units = plan()
    crows = nc.dram_tensor("c_rows", (8, TOK), F32, kind="Internal").ap()
    kept = nc.dram_tensor("x_kept", (4, 128, D), F32, kind="Internal").ap()
    A, V, G, T, SY = nc.scalar, nc.vector, nc.gpsimd, nc.tensor, nc.sync

    with ExitStack() as ctx:
        def sb(name, shape, dt=F32, where=ctx):
            return where.enter_context(nc.sbuf_tensor(name, shape, dt))

        sigs = {}

        def S(name, step=1):
            if name not in sigs:
                sigs[name] = Sig(ctx.enter_context(nc.semaphore("s_" + name)), step)
            return sigs[name]

        def DS(name):
            return S(name, 16)

        pe, act, dve, pool, sp = Lane(), Lane(), Lane(), Lane(), Lane()

        psum = ctx.enter_context(nc.psum_tensor("psum", [128, 8, 512], F32))
        banks = [Bank(psum[:, i, :]) for i in range(8)]

        NR, NH = 3, 2
        raw = sb("raw", [128, NR, UNIT])
        wh = sb("wh", [128, NH, UNIT], F32R)
        wl = sb("wl", [128, NH, UNIT], F32R)
        hh = sb("hh", [128, 8, TOK], F32R)
        hl = sb("hl", [128, 8, TOK], F32R)
        ah = sb("ah", [128, 8, SEQ], F32R)
        al = sb("al", [128, 8, SEQ], F32R)
        ident = sb("ident", [128, 128])
        ones = sb("ones", [128, TOK])
        blk = sb("blk", [128, 2])
        mis = sb("mis", [128, 2112])
        gt = sb("gt", [128, 2, D])
        sgt = sb("sgt", [128, 2056])
        two = sb("two", [128, 2, SEQ])
        tmp = sb("tmp", [128, 2, SEQ])
        cols = sb("cols", [128, 4, 8])
        prm = sb("prm", [128, 56])
        cact = sb("cact", [128, 8])
        half = sb("half", [128, 16])
        sm = sb("sm", [128, 512])
        ccol = sb("ccol", [128, 4, 8])
        acc = mis[:, 0:2048]
        c_ng, c_ps, c_g1, c_g2, c_c, c_gqk, c_bf = (prm[:, 0:8], prm[:, 8:12], prm[:, 12:20], prm[:, 20:28],
                                                    prm[:, 28:36], prm[:, 36:38], prm[:, 38:39])
        for dst, src in ((c_ng, ng), (c_ps, pscale), (c_g1, gn1), (c_g2, gn2), (c_c, cvec), (c_gqk, gqk),
                         (c_bf, bf)):
            t_small = act(A.dma_start, dst, src, s=DS("d_small"))

        pool(G.memset, ones[:, :], 1.0, s=S("p_const"))
        pool(G.memset, half[:, :], -0.5, s=S("p_const"))
        t = pool(G.memset, ident[:, :], 0.0, s=S("p_const"))
        pool(G.affine_select, out=ident[:, :], in_=ident[:, :], compare_op=ALU.not_equal, fill=1.0, base=0,
             pattern=[[-1, 128]], channel_multiplier=1, w=t, s=S("p_const"))
        t = pool(G.memset, blk[:, :], 0.0, s=S("p_const"))
        pool(G.memset, blk[0:64, 0:1], 1.0, w=t, s=S("p_const"))
        t_const = pool(G.memset, blk[64:128, 1:2], 1.0, w=t, s=S("p_const"))

        st = {"dma": 0, "split": 0, "w": 0, "use": 0, "rate": 0, "ring": None,
              "last": sum(u[0] != "ada" for u in units) - 1}
        landed, slot_free, parts_of, done, ada = {}, {}, {}, {}, {"free": None}

        def load():
            n = st["dma"]
            if n < len(units):
                st["dma"] += 1
                landed[n] = sp(SY.dma_start, raw[:, n % NR, :], wall[n], w=slot_free.get(n - NR),
                               s=DS(f"d_w{n % NR}"))

        def ada_unit(n):
            _, _, kt, g = units[n]
            if kt == 0:
                assert "ready" not in ada
                t0 = dve(V.memset, acc, 0.0, w=ada["free"], s=S("v_acc"))
                ada["t"] = sp(SY.dma_start, acc[0:1, :], bada[g:g + 1, :], w=t0, s=DS("d_bada"))
            ada["t"] = dve(V.scalar_tensor_tensor, acc, raw[:, n % NR, :], cact[:, kt:kt + 1], acc, ALU.mult,
                           ALU.add, w=[landed[n], ada["t"], t_cact], s=S("v_acc"))
            slot_free[n] = ada["t"]
            load()
            if kt == 7:
                ada["ready"] = (g, ada["t"])

        def split_next():
            while st["split"] < len(units) and units[st["split"]][0] == "ada":
                st["split"] += 1
                ada_unit(st["split"] - 1)
            n = st["split"]
            if n >= len(units):
                return
            st["split"] += 1
            w = st["w"]
            st["w"] += 1
            r, i, old = raw[:, n % NR, :], w % NH, done.get(w - NH)
            t1 = act(A.activation, wh[:, i, :], r, ACT.Copy, w=[landed[n], old], s=S("a_wh"))
            t2 = dve(V.tensor_tensor, wl[:, i, :], r, wh[:, i, :].bitcast(F32), ALU.subtract, w=[t1, old],
                     s=S("v_wl"))
            parts_of[w] = [t1, t2]
            slot_free[n] = [t1, t2]
            load()

        mod_tok = {}

        def ada_finish():
            if "ready" not in ada:
                return
            ring = st["ring"]
            g, tk = ada.pop("ready")
            ends = []
            for hf in range(2):
                which = 2 * g + hf
                if which in (2, 5):
                    row = gt[:, which // 3, :]
                    for c in range(2):
                        b = ring.next()
                        t = pe(T.matmul, b.ap, ones[:, 0:128], acc[:, 1024 * hf + 512 * c:1024 * hf + 512 * c + 512],
                               start=True, stop=True, w=[tk, b.free, t_const], s=S("t_ada"))
                        t2 = act(A.activation, row[:, 512 * c:512 * c + 512], b.ap, ACT.Copy,
                                 w=[t, st["za"]], s=S("a_ada"))
                        b.free = [t2]
                else:
                    b = ring.next()
                    for c in range(8):
                        o = 1024 * hf + 128 * c
                        t = pe(T.matmul, b.ap[:, 2 * c:2 * c + 2], acc[:, o:o + 128], ones[:, 0:2], start=(c == 0),
                               stop=(c == 7), skip_group_check=True, w=[tk, b.free, t_const], s=S("t_ada"))
                    j = {0: 0, 1: 1, 3: 2, 4: 3}[which]
                    src = b.ap[:, 0:16].rearrange("p (a b) -> p a b", b=2)[:, :, 0]
                    if which in (0, 3):
                        t2 = dve(V.tensor_copy, cols[:, j, :], src, w=t, s=S("v_ada"))
                    else:
                        t2 = dve(V.scalar_tensor_tensor, cols[:, j, :], src, 1.0, c_g1 if which == 1 else c_g2,
                                 ALU.add, ALU.mult, w=[t, t_small], s=S("v_ada"))
                    b.free = [t2]
                ends.append(t)
                mod_tok[which] = t2
            ada["free"] = ends

        queue = []

        def fill(n):
            for _ in range(min(n, len(queue))):
                queue.pop(0)()

        def drain():
            fill(len(queue))

        class Unit:

            def __init__(self):
                w = self.w = st["use"]
                st["use"] += 1
                self.h, self.l = wh[:, w % NH, :], wl[:, w % NH, :]
                while st["w"] <= min(w + 1, st["last"]):
                    split_next()
                self.t = parts_of[w]

            def over(self, t):
                done[self.w] = t
                ada_finish()

        def three(bank, lh, ll, rh, rl, first, last, w=None, s=None):
            pe(T.matmul, bank, lh, rh, start=first, stop=False, skip_group_check=True, w=w)
            pe(T.matmul, bank, lh, rl, start=False, stop=False, skip_group_check=True)
            return pe(T.matmul, bank, ll, rh, start=False, stop=last, skip_group_check=True, s=s)

        def group_cols(u, bank, src, src_tok, sub=0, base=None, nk=8, c0=0, n=SEQ, k0=0):
            for k in range(nk):
                o = (k * 256 + sub * 128) if base is None else base + 128 * k
                t = three(bank.ap[:, 0:n], u.h[:, o:o + 128], u.l[:, o:o + 128], src[0][:, k0 + k, c0:c0 + n],
                          src[1][:, k0 + k, c0:c0 + n], k == 0, k == nk - 1,
                          w=[src_tok[k0 + k], [u.t, bank.free] if k == 0 else None],
                          s=S("t_mm") if k == nk - 1 else None)
                if n == SEQ and k % 2 and k < nk - 1:
                    fill(st["rate"])
            return t

        def group_rows(src, src_tok, tiles, bank_of, evac):
            for kh in range(2):
                u = Unit()
                for i, c0 in enumerate(tiles):
                    b = bank_of[i]
                    for k in range(4):
                        kk = 4 * kh + k
                        t = three(b.ap, src[0][:, kk, c0:c0 + 128], src[1][:, kk, c0:c0 + 128],
                                  u.h[:, 512 * k:512 * k + 512], u.l[:, 512 * k:512 * k + 512], kk == 0, kk == 7,
                                  w=[src_tok[kk], u.t, b.free if kk == 0 else None],
                                  s=S("t_mm") if k == 3 else None)
                    if kh == 1:
                        evac(i, b, t)
                    fill(st["rate"])
                u.over(t)
            return t

        def split_sb(hi, lo, src, w):
            t1 = act(A.activation, hi, src, ACT.Copy, w=w, s=S("a_hi"))
            return [t1, dve(V.tensor_tensor, lo, src, hi.bitcast(F32), ALU.subtract, w=[t1, w], s=S("v_lo"))]

        def rstd(w, i, n, inv, rows=128):
            v = sm[0:rows, i:i + n]
            t = pool(G.tensor_scalar, v, v, inv, EPS, ALU.mult, ALU.add, w=w, s=S("p_ms"))
            return pool(G.tensor_tensor, v, v, half[0:rows, 0:n], ALU.pow, w=[t, t_const], s=S("p_rstd"))

        def square_sum(src, i, w, rows=128):
            j = tmp[0:rows, :, :].rearrange("p a b -> p (a b)")
            return act(A.activation, j, src, ACT.Square, accum_out=sm[0:rows, i:i + 1],
                       w=[w, S("a_sq").now(), S("v_tmp").now()], s=S("a_sq"))

        def transposed(tiles, ring, take):
            toks = []
            for kt in range(8):
                b = ring.next()
                for i, (src, tk) in enumerate(tiles):
                    t = pe(T.transpose, b.ap[:, 128 * i:128 * i + 128], src[:, 128 * kt:128 * kt + 128],
                           ident[:, :], w=[tk, t_const, b.free if i == 0 else None],
                           s=S("t_tp") if i == len(tiles) - 1 else None)
                toks.append(take(kt, b, t))
            return toks

        first = ExitStack()
        xt = sb("xt", [128, 4, D], where=first)
        xm = sb("xm", [META, D], where=first)
        wfb = sb("wfb", [128, 8, 128], where=first)
        wfh = sb("wfh", [128, 8, 128], F32R, where=first)
        wfl = sb("wfl", [128, 8, 128], F32R, where=first)
        fa = sb("fa", [128, TOK], where=first)
        fe = sb("fe", [128, TOK], where=first)
        fc = sb("fc", [128, TOK], where=first)
        t_m = act(A.dma_start, xm[:, :], meta, s=DS("d_xm"))
        t_x = [sp(SY.dma_start, xt[:, i, :], x[128 * i:128 * i + 128, :], s=DS(f"d_x{i}")) for i in range(4)]
        t_wf = act(A.dma_start, wfb[:, :, :], wf, s=DS("d_wf"))
        for _ in range(NR):
            load()

        t = act(A.activation, sm[:, 300:308], c_c, ACT.Sigmoid, w=t_small, s=S("a_c"))
        t_cact = dve(V.tensor_tensor, cact[:, :], c_c, sm[:, 300:308], ALU.mult, w=[t, t_small], s=S("v_c"))

        normed = []
        for i, (src, tk, rows) in enumerate([(xm[:, :], t_m, META)] + [(xt[:, i, :], t_x[i], 128) for i in range(4)]):
            t = square_sum(src, 310 + i, tk, rows)
            r = rstd(t, 310 + i, 1, 1.0 / D, rows)
            t2 = dve(V.tensor_scalar, src, src, sm[0:rows, 310 + i:311 + i], None, ALU.mult, w=r, s=S("v_xn"))
            normed.append((src, t2))
        bm = banks[4]
        for kt in range(8):
            t = pe(T.transpose, bm.ap[:, 16 * kt:16 * kt + 16], xm[:, 128 * kt:128 * kt + 128],
                   ident[0:META, 0:META], w=[normed[0][1], t_const], s=S("t_tp"))
        for kt in range(8):
            t1 = act(A.activation, hh[:, kt, 0:META], bm.ap[:, 16 * kt:16 * kt + 16], ACT.Copy,
                     scale=c_ng[:, kt:kt + 1], w=[t, t_small], s=S("a_hi"))
        for kt in range(8):
            t_hm = dve(V.scalar_tensor_tensor, hl[:, kt, 0:META], bm.ap[:, 16 * kt:16 * kt + 16],
                       c_ng[:, kt:kt + 1], hh[:, kt, 0:META].bitcast(F32), ALU.mult, ALU.subtract, w=[t1, t],
                       s=S("v_lo"))
        bm.free = [t1, t_hm]

        def take_first(kt, b, t):
            g, o = c_ng[:, kt:kt + 1], hh[:, kt, META:TOK]
            t1 = act(A.activation, o, b.ap, ACT.Copy, scale=g, w=t, s=S("a_hi"))
            t2 = dve(V.scalar_tensor_tensor, hl[:, kt, META:TOK], b.ap, g, o.bitcast(F32), ALU.mult,
                     ALU.subtract, w=[t1, t], s=S("v_lo"))
            b.free = [t1, t2]
            return [t1, t2, t_hm]

        h_tok = transposed(normed[1:], Ring(banks[0:4]), take_first)
        hs = (hh, hl)

        tw = split_sb(wfh[:, :, :], wfl[:, :, :], wfb[:, :, :], t_wf)
        fb, fmb = banks[5], banks[6]
        for (b, c0, n) in ((fmb, 0, META), (fb, META, SEQ)):
            for k in range(8):
                t = three(b.ap[:, 0:n], wfh[:, k, :], wfl[:, k, :], hh[:, k, c0:c0 + n], hl[:, k, c0:c0 + n],
                          k == 0, k == 7, w=[tw, h_tok[k]], s=S("t_mm") if k == 7 else None)
        dve(V.tensor_scalar, fa[:, 0:META], fmb.ap[:, 0:META], c_bf, None, ALU.add, w=[t, t_small], s=S("v_f"))
        ta = dve(V.tensor_scalar, fa[:, META:TOK], fb.ap, c_bf, None, ALU.add, w=t, s=S("v_f"))
        fb.free, fmb.free = [ta], [ta]
        tb = act(A.activation, fe[:, :], fa[:, :], ACT.Abs, w=ta, s=S("a_f"))
        tb = act(A.activation, fe[:, :], fe[:, :], ACT.Exp, scale=-1.0, w=tb, s=S("a_f"))
        tb = act(A.activation, fe[:, :], fe[:, :], ACT.Ln, bias=1.0, w=tb, s=S("a_f"))
        ta = dve(V.scalar_tensor_tensor, fa[:, :], fa[:, :], 0.0, fe[:, :], ALU.min, ALU.subtract, w=[ta, tb],
                 s=S("v_f"))
        ta = dve(V.tensor_tensor_scan, fc[:, :], ones[:, :], fa[:, :], 0.0, ALU.mult, ALU.add, w=[ta, t_const],
                 s=S("v_f"))
        t_crow = sp(SY.dma_start, crows, fc[0:8, :], w=ta, s=DS("d_c"))
        first_over = [t_crow, S("t_mm").now()]

        def columns_of_c():
            for i in range(4):
                t = pe(T.transpose, fb.ap[:, 128 * i:128 * i + 128], fc[:, META + 128 * i:META + 128 * i + 128],
                       ident[:, :], w=[ta, fb.free], s=S("t_tp"))
            t2 = dve(V.tensor_copy, ccol[:, :, :], fb.ap.rearrange("p (i c) -> p i c", i=4)[:, :, 0:8], w=t,
                     s=S("v_cc"))
            fb.free = [t2]
            return t, t2

        at_tok, at_free = {}, [None]

        class Att:

            def __init__(self, kind, m, v2, p_sb, pt, tring, obank, sring, ybase):
                self.kind, self.m, self.v2, self.p, self.pt = kind, m, v2, p_sb, pt
                self.tring, self.ob, self.sring, self.ybase = tring, obank, sring, ybase
                self.off = [sum(m + 128 * (j + 1) for j in range(i)) for i in range(4)]
                self.ptoff = {0: 0, 1: 512, 2: 896, 3: 1152, -1: 1280}
                self.qk, self.extra, self.za = {}, {}, {}
                self.pused, self.tok, self.ptt, self.ptused, self.used, self.hi = {}, {}, {}, {}, {}, None
                self.vfree, self.vtok, self.pfree = None, None, None
                self.prepare = None

            def score(self, h, i):
                m, kind, n = self.m, self.kind, 128 * (i + 1)
                if i == 0 and self.prepare:
                    self.prepare(h)
                par = 64 * (h % 2)
                q, k, km, ready = self.qk[h // 2]
                ql = q[par:par + 64, 128 * i:128 * i + 128]
                P = self.p[:, h % 2, self.off[i]:self.off[i] + m + n]
                b = self.sring.next()
                if m:
                    pe(T.matmul, b.ap[:, 512 - m:512], ql, km[par:par + 64, :], start=True, stop=True,
                       skip_group_check=True, w=[ready, b.free])
                    sc, rb = b.ap[:, 512 - m:512 + n], b.ap[:, 512:512 + n]
                else:
                    sc = rb = b.ap[:, 0:n]
                t = pe(T.matmul, rb, ql, k[par:par + 64, 0:n], start=True, stop=True, skip_group_check=True,
                       w=[ready, b.free], s=S("t_sc"))
                old_p = [self.pused.get(h - 2), self.pfree]
                c = 320 + 4 * ((4 * h + i) % 16)
                mx, su, nmx = sm[:, c:c + 1], sm[:, c + 1:c + 2], sm[:, c + 2:c + 3]
                old = self.tok.get(4 * h + i - 16)
                diag = P[:, m + n - 128:m + n]
                if kind == "sb":
                    g = self.extra[(4 * h + i) % 2]
                    gg = g["ap"][:, 512 - n:512]
                    t1 = act(A.activation, P, sc, ACT.Sigmoid, w=[t, old_p], s=S("a_s"))
                    t1b = act(A.activation, gg, sc, ACT.Sigmoid, scale=-1.0, w=g["free"], s=S("a_s"))
                    b.free = [t1b]
                    t2a = pool(G.affine_select, out=diag, in_=diag, compare_op=ALU.is_gt, fill=0.0, base=0,
                               pattern=[[-1, 128]], channel_multiplier=1, w=t1, s=S("p_s"))
                    gd = g["ap"][:, 384:512]
                    t2 = pool(G.affine_select, out=gd, in_=gd, compare_op=ALU.is_gt, fill=1.0, base=0,
                              pattern=[[-1, 128]], channel_multiplier=1, w=t1b, s=S("p_s"))
                    yield
                    t3 = dve(V.tensor_tensor_scan, gg[:, ::-1], gg[:, ::-1], ones[:, 0:n], 1.0, ALU.mult, ALU.mult,
                             w=[t2, t1b, t_const], s=S("v_s"))
                    yield
                    t4 = dve(V.tensor_tensor, P, P, g["ap"][:, 513 - n:513], ALU.mult, w=[t3, t2, g["one"]],
                             s=S("v_p"))
                    g["free"] = [t4]
                    self.tok[4 * h + i] = t4
                    return
                if kind == "fg":
                    cb, cbt = self.extra[h]
                    t1 = dve(V.scalar_tensor_tensor, P, sc, ccol[:, i, h:h + 1], cb[:, 0:m + n], ALU.add,
                             ALU.subtract, w=[t, old_p, cbt, t_cc], s=S("v_s"))
                    t2 = pool(G.affine_select, out=diag, in_=diag, compare_op=ALU.is_ge, fill=NEG, base=0,
                              pattern=[[-1, 128]], channel_multiplier=1, w=t1, s=S("p_s"))
                    yield
                    t3 = dve(V.tensor_reduce, nmx, P, AX.X, ALU.max, negate=True, w=[t2, old], s=S("v_m"))
                else:
                    bt, btt = self.extra[h]
                    t1 = dve(V.tensor_tensor_reduce, out=P, in0=sc, in1=bt[:, 512 - n:512], scale=1.0,
                             scalar=-3.0e38, op0=ALU.add, op1=ALU.max, accum_out=mx, w=[t, old_p, btt, old],
                             s=S("v_s"))
                    yield
                    t3 = dve(V.tensor_scalar, nmx, mx, -1.0, None, ALU.mult, w=t1, s=S("v_m"))
                b.free = [t1]
                self.used[h] = t1
                t4 = act(A.activation, P, P, ACT.Exp, bias=nmx, accum_out=su, w=[t3, t1, t2 if m else None],
                         s=S("a_s"))
                yield
                t5 = dve(V.reciprocal, mx, su, w=t4, s=S("v_m"))
                self.tok[4 * h + i] = act(A.activation, P, P, ACT.Copy, scale=mx, w=[t5, t4], s=S("a_p"))

            def turn(self, h, j):
                b = self.tring.next()
                i0, rows, w = max(j, 0), (128 if j >= 0 else META), 512 - 128 * max(j, 0)
                for i in range(i0, 4):
                    o = self.off[i] + (self.m + 128 * j if j >= 0 else 0)
                    t = pe(T.transpose, b.ap[:, 128 * (i - i0):128 * (i - i0) + 128], self.p[:, h % 2, o:o + 128],
                           ident[:, :], w=[self.tok[4 * h + i], b.free if i == i0 else None],
                           s=S("t_tp") if i == 3 else None)
                if j == 3:
                    self.pused[h] = t
                o = self.ptoff[j]
                ph, pl = self.pt
                old = [self.ptused.get(j), self.pfree]
                t1 = act(A.activation, ph[0:rows, o:o + w], b.ap[0:rows, 0:w], ACT.Copy, w=[t, old], s=S("a_pt"))
                t2 = dve(V.tensor_tensor, pl[0:rows, o:o + w], b.ap[0:rows, 0:w], ph[0:rows, o:o + w].bitcast(F32),
                         ALU.subtract, w=[t1, t, old], s=S("v_pt"))
                b.free = [t1, t2]
                self.ptt[j] = [t1, t2]

            def value(self, h, j):
                i0, rows, w, o = max(j, 0), (128 if j >= 0 else META), 512 - 128 * max(j, 0), self.ptoff[j]
                ph, pl = self.pt
                lhs = self.v2[0:rows, (j if j >= 0 else 4), h, :]
                b, start = self.ob, (j == -1) if self.m else (j == 0)
                pe(T.matmul, b.ap[:, 128 * i0:512], lhs, ph[0:rows, o:o + w], start=start, stop=False,
                   skip_group_check=True, w=[self.ptt[j], self.vtok, b.free if start else None])
                t = pe(T.matmul, b.ap[:, 128 * i0:512], lhs, pl[0:rows, o:o + w], start=False, stop=(j == 3),
                       skip_group_check=True, s=S("t_pv"))
                self.ptused[j] = t
                if j == 3:
                    par = 64 * (h % 2)
                    t1 = act(A.activation, tmp[0:64, 0, :], b.ap[64:128, :], ACT.Copy,
                             w=[t, S("v_tmp").now(), S("a_sq").now()], s=S("a_o"))
                    t2 = dve(V.tensor_tensor, tmp[par:par + 64, 1, :], b.ap[0:64, :], tmp[0:64, 0, :], ALU.add,
                             w=[t1, t, self.hi], s=S("v_tmp"))
                    b.free = [t1, t2]
                    if par:
                        o = tmp[:, 1, :]
                        if self.kind == "fg":
                            z, zt = self.za[h // 2]
                            t2 = dve(V.tensor_tensor, o, o, z, ALU.mult, w=[t2, zt], s=S("v_tmp"))
                        p = self.ybase + h // 2
                        self.hi = at_tok[p] = split_sb(ah[:, p, :], al[:, p, :], o, [t2, at_free[0]])

            def steps(self, heads):
                pend, out_ = [], []

                def flush():
                    for g in list(pend):
                        if next(g, True):
                            pend.remove(g)

                def step(fn):
                    out_.append(fn)

                def sc(h, i):
                    def run():
                        flush()
                        g = self.score(h, i)
                        next(g)
                        pend.append(g)
                    return run

                def tv(fn, h, j):
                    def run():
                        flush()
                        fn(h, j)
                    return run

                rounds = ([-1] if self.m else []) + [0, 1, 2, 3]
                for i in range(4):
                    step(sc(heads[0], i))
                for a, h in enumerate(heads):
                    step(flush)
                    step(flush)
                    step(flush)
                    for r, j in enumerate(rounds):
                        step(tv(self.turn, h, j))
                        i = r - len(rounds) + 4
                        if a + 1 < len(heads) and i >= 0:
                            step(sc(heads[a + 1], i))
                        if r:
                            step(tv(self.value, h, rounds[r - 1]))
                    step(tv(self.value, h, 3))
                return out_

        def value_parts(att, rows_of):
            def evac(i, b, t):
                r = rows_of[i]
                src = b.ap[0:r, :].rearrange("p (h c) -> p h c", h=8)
                hi, lo = att.v2[0:r, i, :, 0:64], att.v2[0:r, i, :, 64:128]
                t1 = act(A.activation, hi, src, ACT.Copy, w=[t, att.vfree], s=S("a_hi"))
                t2 = dve(V.tensor_tensor, lo, src, hi.bitcast(F32), ALU.subtract, w=[t1, t, att.vfree],
                         s=S("v_lo"))
                b.free = [t1, t2]
                att.vtok = [t1, t2]
            return evac

        ub, us, pw = mis[:, 0:528], (mis[:, 528:1056], mis[:, 1056:1584]), mis[:, 1584:2096]
        za = gt.rearrange("p a b -> p (a b)").rearrange("p (a b) -> p a b", a=4)
        zp = two
        t_pw = act(A.dma_start, pw, poolw, s=DS("d_pw"))
        t_cp, t_cc = columns_of_c()
        first_over += [t_cp]
        first.close()

        b1 = ExitStack()
        v2 = sb("v2", [128, 5, 8, 128], F32R, where=b1)
        p_sb = sb("p_sb", [128, 2, 4 * META + 1280], where=b1)
        pth = sb("pth", [128, 1280 + SEQ], F32R, where=b1)
        ptl = sb("ptl", [128, 1280 + SEQ], F32R, where=b1)
        q_sb = sb("q_sb", [128, 2, SEQ], where=b1)
        k_sb = sb("k_sb", [128, 2, SEQ], where=b1)
        km_sb = sb("km_sb", [128, 2, META], where=b1)
        cb = sb("cb", [128, 2, TOK], where=b1)

        sbank = Bank(psum[:, 4:6, :].rearrange("p a b -> p (a b)"))
        tring = Ring([banks[3], banks[6]])
        fg = Att("fg", META, v2, p_sb, (pth, ptl), tring, banks[7], Ring([sbank]), 4)
        fg.vfree = fg.pfree = first_over

        def row_of_c(h):
            i = h % 2
            fg.extra[h] = (cb[:, i, :], sp(SY.dma_start, cb[:, i, :], crows[h:h + 1, :].to_broadcast([128, TOK]),
                                           w=[t_crow, first_over, fg.used.get(h - 2)], s=DS(f"d_cb{i}")))
        fg.prepare = row_of_c

        group_rows(hs, h_tok, [META, META + 128, META + 256, META + 384, 0], banks[0:4] + [banks[7]],
                   value_parts(fg, [128, 128, 128, 128, META]))
        sbank.free = banks[4].free + banks[5].free
        pr = Ring(banks[0:3])

        def gate(dst, b, t, w):
            t1 = act(A.activation, dst, b.ap, ACT.Sigmoid, w=[t, w], s=S("a_z"))
            t2 = dve(V.tensor_tensor, dst, b.ap, dst, ALU.mult, w=[t1, t], s=S("v_z"))
            b.free = [t1, t2]
            return t2

        for j in range(2):
            u = Unit()
            for sub in range(2):
                b = pr.next()
                t = group_cols(u, b, hs, h_tok, sub, c0=META)
                fg.za[2 * j + sub] = (za[:, 2 * j + sub, :], gate(za[:, 2 * j + sub, :], b, t, None))
            u.over(t)

        def meta_cols(u, sub, dst, w):
            b = tring.next()
            t = group_cols(u, b, hs, h_tok, sub, c0=0, n=META)
            b.free = [act(A.activation, dst, b.ap[:, 0:META], ACT.Copy, w=[t, w], s=S("a_m"))]
            return b.free[0], t

        us_used = ub_used = None
        zp_used = {}
        st["rate"] = 2
        for p in range(4):
            i = p % 2
            u = Unit()
            old = [S("t_sc").now(), first_over]
            b = pr.next()
            t = group_cols(u, b, hs, h_tok, 0, c0=META)
            tq = act(A.activation, q_sb[:, i, :], b.ap, ACT.Copy, scale=0.125, w=[t, old], s=S("a_q"))
            b.free = [tq]
            b = pr.next()
            t = group_cols(u, b, hs, h_tok, 1, c0=META)
            tk = act(A.activation, k_sb[:, i, :], b.ap, ACT.Copy, w=[t, old], s=S("a_q"))
            b.free = [tk]
            tm, t = meta_cols(u, 1, km_sb[:, i, :], old)
            u.over(t)
            drain()
            fg.qk[p] = (q_sb[:, i, :], k_sb[:, i, :], km_sb[:, i, :], [tq, tk, tm])
            queue.extend(fg.steps([2 * p, 2 * p + 1]))

            u = Unit()
            b = pr.next()
            t = group_cols(u, b, hs, h_tok, 0, c0=META)
            tu1 = act(A.activation, ub[:, META:TOK], b.ap, ACT.Copy, w=[t, ub_used], s=S("a_m"))
            b.free = [tu1]
            tu, t = meta_cols(u, 0, ub[:, 0:META], ub_used)
            b = pr.next()
            t = group_cols(u, b, hs, h_tok, 1, c0=META)
            u.over(t)
            yo = zp[:, i, :]
            tz = gate(yo, b, t, zp_used.get(p - 2))
            src, lo, tt = ub, 0, [tu, tu1, us_used]
            for s_ in range(p + 1):
                dst, dd = us[s_ % 2], 1 << s_
                lo += dd
                tt = dve(V.tensor_tensor, dst[:, lo:TOK], src[:, lo:TOK], src[:, lo - dd:TOK - dd], ALU.add,
                         w=tt, s=S("v_u"))
                src = dst
            pd = us[(p + 1) % 2][:, META:TOK]
            tt = dve(V.scalar_tensor_tensor, pd, src[:, META:TOK], 1.0 / (2 << p), ub[:, META:TOK], ALU.mult,
                     ALU.subtract, w=tt, s=S("v_u"))
            ub_used = tt
            fill(3)
            b = pr.next()
            t = pe(T.matmul, b.ap, pw[:, 128 * p:128 * p + 128], pd, start=True, stop=True,
                   w=[tt, t_pw, b.free], s=S("t_y"))
            us_used = t
            t3 = dve(V.scalar_tensor_tensor, yo, b.ap, c_ps[:, p:p + 1], yo, ALU.mult, ALU.mult, w=[t, tz],
                     s=S("v_y"))
            b.free = [t3]
            zp_used[p] = at_tok[p] = split_sb(ah[:, p, :], al[:, p, :], yo, t3)
        ada["free"] = [us_used, tt]

        sg = sgt[:, 0:2048].rearrange("p (a b) -> p a b", a=4)
        mt = two
        sg_used, mt_used, m_tok, mm_parts = {}, zp_used[3], {}, None
        for e_ in range(4):
            sgo = {}
            for dd in range(2):
                u = Unit()
                for sub in range(2):
                    b = pr.next()
                    t = group_cols(u, b, hs, h_tok, sub, c0=META)
                    n = 2 * dd + sub
                    sgo[n] = act(A.activation, sg[:, n, :], b.ap, ACT.Sigmoid, w=[t, sg_used.get(n)], s=S("a_g"))
                    b.free = [sgo[n]]
                u.over(t)
            if e_ == 0:
                drain()
                st["rate"] = 0
                b1.close()
                b1_over = [S("t_pv").now(), S("t_tp").now(), S("a_pt").now(), S("v_pt").now(), at_tok[7],
                           S("v_s").now()]
                st["za"] = at_tok[7]
                w1 = ExitStack()
                x1 = sb("x1", [128, 4, D], where=w1)
                gf = sb("gf", [128, D], where=w1)
                w1a = ExitStack()
                mh = sb("mh", [128, 8, SEQ], F32R, where=w1a)
                ml = sb("ml", [128, 8, SEQ], F32R, where=w1a)
                t_x1 = [sp(SY.dma_start, x1[:, i, :], x[128 * i:128 * i + 128, :], w=b1_over, s=DS(f"d_x{i}"))
                        for i in range(4)]
                t_gf = sp(SY.dma_start, gf[:, :], fng.to_broadcast([128, D]), w=b1_over, s=DS("d_gf"))
                st["ring"] = Ring([banks[3], banks[6]])
            u = Unit()
            for dd in range(2):
                n = 2 * e_ + dd
                b = pr.next()
                t = group_cols(u, b, (ah, al), at_tok, base=dd * 1024, nk=4)
                t1 = dve(V.tensor_tensor, mt[:, 0, :], b.ap, sg[:, 2 * dd, :], ALU.mult,
                         w=[t, sgo[2 * dd], mt_used], s=S("v_m1"))
                b.free = [t1]
                b = pr.next()
                t = group_cols(u, b, (ah, al), at_tok, base=dd * 1024 + 512, nk=4, k0=4)
                t2 = dve(V.tensor_tensor, mt[:, 1, :], b.ap, sg[:, 2 * dd + 1, :], ALU.mult,
                         w=[t, sgo[2 * dd + 1], mt_used], s=S("v_m1"))
                b.free = [t2]
                sg_used[2 * dd], sg_used[2 * dd + 1] = t1, t2
                t3 = dve(V.tensor_tensor, mt[:, 0, :], mt[:, 0, :], mt[:, 1, :], ALU.add, w=[t1, t2], s=S("v_m1"))
                mt_used = m_tok[n] = split_sb(mh[:, n, :], ml[:, n, :], mt[:, 0, :], [t3, b1_over])
            u.over(t)
        at_free[0] = t

        t1s = {}

        def evac_out(ch):
            def evac(i, b, t):
                o = x1[:, i, 512 * ch:512 * ch + 512]
                t1s[i, ch] = dve(V.tensor_tensor, o, b.ap, o, ALU.add, w=[t, t_x1[i]], s=S("v_r"))
                b.free = [t1s[i, ch]]
            return evac

        for ch in range(2):
            bk = banks[0:4] if ch == 0 else [banks[4], banks[5], banks[7], banks[3]]
            st["ring"] = Ring([banks[6]])
            if ch == 0:
                for b in (banks[4], banks[5]):
                    b.free = b.free + sbank.free
            t = group_rows((mh, ml), m_tok, [0, 128, 256, 384], bk, evac_out(ch))
        w1a.close()
        xn = sb("xn", [128, 4, D], where=w1)
        m_over = t
        normed = []
        t_kept = []
        for i in range(4):
            xi = x1[:, i, :]
            t = square_sum(xi, 384 + i, [t1s[i, 0], t1s[i, 1]])
            r = rstd(t, 384 + i, 1, 1.0 / D)
            t = dve(V.scalar_tensor_tensor, xi, xi, sm[:, 384 + i:385 + i], gf[:, :], ALU.mult, ALU.mult,
                    w=[r, t_gf, t1s[i, 1]], s=S("v_xn"))
            t_kept.append(sp(SY.dma_start, kept[i], xi, w=t, s=DS(f"d_k{i}")))
            t2 = square_sum(xi, 388 + i, t)
            r = rstd(t2, 388 + i, 1, 1.0 / D)
            t = dve(V.tensor_scalar, xn[:, i, :], xi, sm[:, 388 + i:389 + i], None, ALU.mult, w=[r, m_over, t],
                    s=S("v_xn"))
            normed.append((xn[:, i, :], t))

        def take_mod(j, old):
            def take(kt, b, t):
                o, d = kt % 2, two[:, kt % 2, :]
                t0 = dve(V.tensor_scalar, d, b.ap, cols[:, j + 1, kt:kt + 1], cols[:, j, kt:kt + 1], ALU.mult,
                         ALU.add, w=[t, mod_tok[{0: 0, 2: 3}[j]], mod_tok[{0: 1, 2: 4}[j]], two_used[o]],
                         s=S("v_two"))
                b.free = [t0]
                two_used[o] = split_sb(hh[:, kt, 0:SEQ], hl[:, kt, 0:SEQ], d, [t0, old])
                return two_used[o]
            return take

        two_used = [mt_used, mt_used]
        h_tok = transposed(normed, Ring(banks[0:4]), take_mod(0, m_over))
        x1_over = [t_kept, S("t_tp").now(), S("a_sq").now(), S("v_xn").now()]
        w1.close()

        b2 = ExitStack()
        v_ca = sb("v_ca", [128, 4, 8, 128], F32R, where=b2)
        v_sb = sb("v_sb", [128, 4, 8, 128], F32R, where=b2)
        p_sb = sb("p_sb2", [128, 2, 1280], where=b2)
        pth = sb("pth2", [128, 1280], F32R, where=b2)
        ptl = sb("ptl2", [128, 1280], F32R, where=b2)
        q_sb = sb("q_sb2", [128, 2, SEQ], where=b2)
        k_sb = sb("k_sb2", [128, 2, SEQ], where=b2)
        bt = (sgt[:, 0:512], sgt[:, 512:1024])
        gb = (sgt[:, 1024:1537], sgt[:, 1538:2051])
        sq = two

        pr = Ring(banks[0:3])
        tring = Ring([banks[3], banks[6]])
        sring = Ring([banks[4], banks[5]])
        ca = Att("ca", 0, v_ca, p_sb, (pth, ptl), tring, banks[7], sring, 4)
        sbk = Att("sb", 0, v_sb, p_sb, (pth, ptl), tring, banks[7], sring, 0)
        for a_ in (ca, sbk):
            a_.vfree = a_.pfree = x1_over
        relo = {"t": None}

        def table(h):
            i = h % 2
            t = sp(SY.dma_start, bt[i], rel[h], w=[sg_used[0], sg_used[1], ca.used.get(h - 2)], s=DS(f"d_bt{i}"))
            ca.extra[h] = (bt[i], pool(G.memset, bt[i][0:64, 448:512], NEG, w=t, s=S("p_bt")))
        ca.prepare = table

        hs2 = (hh, hl)
        group_rows(hs2, h_tok, [0, 128, 256, 384], [banks[4], banks[5], banks[7], banks[6]],
                   value_parts(ca, [128] * 4))
        st["rate"] = 4
        qk_used = {}
        tone = [pool(G.memset, gb[i][:, 512:513], 1.0, w=[sg_used[2], sg_used[3]], s=S("p_bt")) for i in range(2)]
        for kind in ("ca", "sb"):
            att = ca if kind == "ca" else sbk
            if kind == "sb":
                vb = [banks[0], banks[1], banks[2], banks[3]]
                tring2 = Ring([banks[6]])
                ca.tring = tring2
                group_rows(hs2, h_tok, [0, 128, 256, 384], vb, value_parts(sbk, [128] * 4))
                drain()
                sbk.pused[-2], sbk.pused[-1] = ca.pused[6], ca.pused[7]
                sbk.ptused = dict(ca.ptused)
                sbk.hi = ca.hi
                sbk.extra = {i: {"ap": gb[i], "free": None, "one": tone[i]} for i in range(2)}
            for p in range(4):
                i = p % 2
                u = Unit()
                old = [S("t_sc").now(), x1_over]
                got = []
                for sub in range(2):
                    dst = (q_sb if sub == 0 else k_sb)[:, i, :]
                    b = pr.next()
                    t = group_cols(u, b, hs2, h_tok, sub)
                    if kind == "ca":
                        ts = act(A.activation, sq[:, sub, :], b.ap, ACT.Square, w=[t, two_used[sub], relo["t"]],
                                 s=S("a_sqk"))
                        t1 = dve(V.tensor_scalar, dst, b.ap, c_gqk[:, sub:sub + 1], 0.125 if sub == 0 else 1.0,
                                 ALU.mult, ALU.mult, w=[t, ts, old, t_small], s=S("v_q"))
                        b.free = [ts, t1]
                        got.append((ts, t1))
                    else:
                        t1 = act(A.activation, dst, b.ap, ACT.Copy, scale=0.125 if sub == 0 else 1.0, w=[t, old],
                                 s=S("a_q"))
                        b.free = [t1]
                        got.append(t1)
                u.over(t)
                if kind == "ca":
                    b = tring.next()
                    for sub in range(2):
                        for tt_ in range(4):
                            c = 8 * sub + 2 * tt_
                            t = pe(T.matmul, b.ap[:, c:c + 2], sq[:, sub, 128 * tt_:128 * tt_ + 128], blk[:, :],
                                   start=(c == 0), stop=(c == 14), skip_group_check=True,
                                   w=[got[sub][0], b.free, t_const], s=S("t_ss"))
                    relo["t"] = t
                    t1 = dve(V.tensor_copy, sm[:, 400:416], b.ap[:, 0:16], w=[t, S("v_ss").now()], s=S("v_ss"))
                    b.free = [t1]
                    r = rstd(t1, 400, 16, 1.0 / 64)
                    drain()
                    rdy = []
                    wide = mis[:, 0:1024].rearrange("p (c f) -> p c f", f=64)
                    r = dve(V.tensor_copy, wide, sm[:, 400:416].unsqueeze(2).to_broadcast([128, 16, 64]),
                            w=[r, relo.get("used"), ada["free"]], s=S("v_ss"))
                    for sub in range(2):
                        dst = (q_sb if sub == 0 else k_sb)[:, i, :]
                        b = pr.next()
                        for tt_ in range(4):
                            c = 64 * (8 * sub + 2 * tt_)
                            lhs = mis[:, c:c + 128]
                            t = pe(T.matmul, b.ap[:, 128 * tt_:128 * tt_ + 128], lhs, ident[:, :], start=(tt_ == 0),
                                   stop=(tt_ == 3), skip_group_check=True, w=[r, b.free, t_const], s=S("t_ss"))
                        t1 = dve(V.tensor_tensor, dst, dst, b.ap, ALU.mult, w=[t, got[sub][1]], s=S("v_q"))
                        b.free = [t1]
                        rdy.append(t1)
                    relo["used"] = t
                else:
                    drain()
                    rdy = got
                att.qk[p] = (q_sb[:, i, :], k_sb[:, i, :], None, rdy)
                queue.extend(att.steps([2 * p, 2 * p + 1]))
        drain()
        st["rate"] = 0
        b2.close()
        b2_over = [S("t_pv").now(), S("t_tp").now(), S("a_pt").now(), S("v_pt").now(), at_tok[3]]

        w2 = ExitStack()
        x1 = sb("x1b", [128, 4, D], where=w2)
        xn = sb("xnb", [128, 4, D], where=w2)
        t_x1 = [sp(SY.dma_start, x1[:, i, :], kept[i], w=[b2_over, t_kept], s=DS(f"d_x{i}")) for i in range(4)]
        tmp_used = {0: S("v_tmp").now(), 1: at_tok[3]}
        res = {}

        def add_gated(j, ch):
            def evac(i, b, t):
                o = x1[:, i, 512 * ch:512 * ch + 512]
                d = tmp[:, i % 2, :]
                t1 = dve(V.tensor_tensor, d, b.ap, gt[:, j, 512 * ch:512 * ch + 512], ALU.mult,
                         w=[t, mod_tok[{0: 2, 1: 5}[j]], tmp_used[i % 2], S("a_sq").now()], s=S("v_tmp"))
                b.free = [t1]
                res[i, ch] = tmp_used[i % 2] = dve(V.tensor_tensor, o, o, d, ALU.add,
                                                   w=[t1, t_x1[i], res.get((i, ch))], s=S("v_tmp"))
            return evac

        for ch in range(2):
            t = group_rows((ah, al), at_tok, [0, 128, 256, 384], banks[4 * ch:4 * ch + 4], add_gated(0, ch))
        at_free[0] = t
        h_over = S("t_mm").now()
        normed = []
        for i in range(4):
            xi = x1[:, i, :]
            t = square_sum(xi, 420 + i, [res[i, 0], res[i, 1]])
            r = rstd(t, 420 + i, 1, 1.0 / D)
            t = dve(V.tensor_scalar, xn[:, i, :], xi, sm[:, 420 + i:421 + i], None, ALU.mult,
                    w=[r, b2_over], s=S("v_xn"))
            normed.append((xn[:, i, :], t))
        two_used = [relo["t"], relo["t"]]
        h_tok = transposed(normed, Ring(banks[0:4]), take_mod(2, h_over))

        r_sb = two
        tmp_used = {0: S("a_sq").now(), 1: S("a_sq").now()}
        pr = Ring(banks[0:4])
        r_used = list(two_used)
        a_old = at_free[0]
        s2 = (sgt[:, 0:512], sgt[:, 512:1024])
        s_used = [[ca.used[6], ca.used[7]]] * 2
        t_out = []
        for q in range(4):
            for j in range(4):
                u = Unit()
                for sub in range(2):
                    n = 2 * j + sub
                    b = pr.next()
                    t = group_cols(u, b, hs2, h_tok, sub)
                    t1 = act(A.activation, r_sb[:, sub, :], b.ap, ACT.Relu, w=[t, r_used[sub]], s=S("a_r"))
                    t2 = dve(V.scalar_tensor_tensor, s2[sub], b.ap, 0.0, r_sb[:, sub, :], ALU.max, ALU.mult,
                             w=[t1, t, s_used[sub]], s=S("v_r2"))
                    r_used[sub] = t2
                    b.free = [t1, t2]
                    s_used[sub] = at_tok[n] = split_sb(ah[:, n, :], al[:, n, :], s2[sub], [t2, a_old])
                u.over(t)
            for ch in range(2):
                bk = banks[4:8] if ch == 0 else banks[0:4]
                evac = add_gated(1, ch)

                def last(i, b, t, evac=evac, ch=ch):
                    evac(i, b, t)
                    t_out.append(act(A.dma_start, out[128 * i:128 * i + 128, 512 * ch:512 * ch + 512],
                                     x1[:, i, 512 * ch:512 * ch + 512], w=res[i, ch], s=DS("d_out")))
                t = group_rows((ah, al), at_tok, [0, 128, 256, 384], bk, last if q == 3 else evac)
            a_old = t
        w2.close()

        block = ctx.enter_context(nc.Block())

        @block.sync
        def _(eng):
            sp.run(eng)
            eng.wait_ge(t_crow[0].sem, t_crow[1])
            for s_, v in t_kept:
                eng.wait_ge(s_.sem, v)

        @block.scalar
        def _(eng):
            act.run(eng)
            eng.wait_ge(t_out[-1][0].sem, t_out[-1][1])

        @block.vector
        def _(eng):
            dve.run(eng)

        @block.gpsimd
        def _(eng):
            pool.run(eng)

        @block.tensor
        def _(eng):
            pe.run(eng)


def kernel(x, meta_tokens, norm_g, w_in, b_forget, pool_w, pool_scale, w_up_pool, w_up_attn, w_out, final_norm_g,
           c_2, g_norm1_2, w_in_2, g_q_2, g_k_2, rel_bias_2, w_o_2, g_norm2_2, w1_2, w2_2, w_ada_2, b_ada_2):
    import numpy as np
    import concourse.bacc as bacc
    from concourse.bass_utils import run_bass_kernel_spmd

    a = {n: np.asarray(v)[0] for n, v in dict(w_in=w_in, w_out=w_out, w_in_2=w_in_2, w_o_2=w_o_2, w1_2=w1_2,
                                              w2_2=w2_2, w_ada_2=w_ada_2, up=w_up_pool, ua=w_up_attn).items()}

    def columns(v):
        return np.ascontiguousarray(np.asarray(v).reshape(-1, 128).T)

    def packed(unit):
        kind, name, p, q = unit
        if kind == "cols":
            w = a[name]
            both = np.concatenate([w[:, p:p + 128], w[:, q:q + 128]], 1)
            return both.reshape(8, 128, 256).transpose(1, 0, 2).reshape(128, UNIT)
        if kind == "rows":
            return a[name][512 * p:512 * p + 512, q:q + 512].reshape(4, 128, 512).transpose(1, 0, 2).reshape(128, UNIT)
        if kind == "ada":
            return a[name][128 * p:128 * p + 128, UNIT * q:UNIT * q + UNIT]
        tiles = [a[s][:, 128 * d:128 * d + 128].reshape(4, 128, 128).transpose(1, 0, 2).reshape(128, 512)
                 for d in (2 * p, 2 * p + 1) for s in ("up", "ua")]
        return np.concatenate(tiles, 1)

    f = np.tile(a["w_in"][:, C_F:C_F + 8], (1, 16)).reshape(8, 128, 128).transpose(1, 0, 2)
    far = np.clip(384 + np.arange(128)[:, None] - np.arange(512)[None, :], -128, 128) + 128
    rel = np.asarray(rel_bias_2)[0][:, far]
    arrays = {
        "x": np.asarray(x)[0],
        "meta": np.asarray(meta_tokens),
        "wall": np.stack([packed(u) for u in plan()]),
        "wf": f,
        "bf": np.tile(np.asarray(b_forget)[0], 16).reshape(128, 1),
        "poolw": np.asarray(pool_w)[0].transpose(1, 0, 2).reshape(128, 512),
        "pscale": columns(np.asarray(pool_scale)[0]),
        "ng": columns(np.asarray(norm_g)[0]),
        "fng": np.asarray(final_norm_g).reshape(1, D),
        "cvec": columns(np.asarray(c_2)[0]),
        "bada": np.asarray(b_ada_2)[0].reshape(3, UNIT),
        "gn1": columns(np.asarray(g_norm1_2)[0]),
        "gn2": columns(np.asarray(g_norm2_2)[0]),
        "gqk": np.stack([np.tile(np.asarray(g_q_2)[0], 2), np.tile(np.asarray(g_k_2)[0], 2)], 1),
        "rel": rel,
    }
    arrays = {n: np.ascontiguousarray(v) for n, v in arrays.items()}
    nc = bacc.Bacc("TRN2", target_bir_lowering=False, num_devices=1, dynamic_dma_scratch_size=1024)
    args = [nc.dram_tensor("in_" + n, v.shape, mybir.dt.from_np(v.dtype), kind="ExternalInput").ap()
            for n, v in arrays.items()]
    out = nc.dram_tensor("out", (SEQ, D), F32, kind="ExternalOutput").ap()
    program(nc, *args, out)
    r = run_bass_kernel_spmd(nc, [{"in_" + n: v for n, v in arrays.items()}], core_ids=[0])
    return r.results[0]["out"].reshape(1, SEQ, D)
```

```python
from contextlib import ExitStack

import concourse.bass as bass
from concourse import mybir

F32 = mybir.dt.float32
F32R = mybir.dt.float32r
ALU = mybir.AluOpType
ACT = mybir.ActivationFunctionType
AX = mybir.AxisListType

D = 1024
SEQ = 512
META = 16
TOK = META + SEQ
UNIT = 2048
RATE_CA, RATE_SB, RATE_WO = 1.5, 2, 2.5
NEG = -1.0e30
EPS = 1e-6

C_U, C_ZP, C_Q, C_K, C_V, C_ZA, C_F, C_GP, C_GA = 0, 512, 1024, 1536, 2048, 2560, 3072, 3080, 4104


ORDER_1 = (("qk", 0), ("qk", 1), ("uz", 0), ("qk", 2), ("uz", 1), ("qk", 3), ("uz", 2), ("uz", 3))


def plan():
    ada = [("ada", "w_ada_2", kt, g) for g in range(3) for kt in range(8)]
    out = [("rows", "w_in", kh, C_V) for kh in range(2)]
    out += [("cols", "w_in", C_ZA + 256 * j, C_ZA + 256 * j + 128) for j in range(2)]
    for kind, p in ORDER_1:
        out.append(("cols", "w_in", (C_Q if kind == "qk" else C_U) + 128 * p, (C_K if kind == "qk" else C_ZP) + 128 * p))
    for e in range(4):
        n = (1, 2, 2) if e == 3 else (2, 1, 2)
        for i, d in enumerate((2 * e, 2 * e + 1)):
            out.append(("cols", "w_in", C_GP + 128 * d, C_GA + 128 * d))
            out += [ada.pop(0) for _ in range(n[i])]
        out.append(("up", "", e, 0))
        out += [ada.pop(0) for _ in range(n[2])]
    for ch in range(2):
        for kh in range(2):
            out.append(("rows", "w_out", kh, 512 * ch))
            out.append(ada.pop(0))
    out += [("rows", "w_in_2", kh, 2560) for kh in range(2)]
    for p in range(4):
        out.append(("cols", "w_in_2", 1536 + 128 * p, 2048 + 128 * p))
    out += [("rows", "w_in_2", kh, 1024) for kh in range(2)]
    for p in range(4):
        out.append(("cols", "w_in_2", 128 * p, 512 + 128 * p))
    for ch in range(2):
        for kh in (1, 0):
            out.append(("rows", "w_o_2", kh, 512 * ch))
    for q in range(4):
        for j in range(4):
            out.append(("cols", "w1_2", 1024 * q + 256 * j, 1024 * q + 256 * j + 128))
        for ch in range(2):
            for kh in range(2):
                out.append(("rows", "w2_2", 2 * q + kh, 512 * ch))
    assert not ada
    return out


class Sig:

    def __init__(self, sem, step):
        self.sem, self.step, self.n = sem, step, 0

    def now(self):
        return (self, self.n)


class Lane:

    def __init__(self):
        self.ops, self.seen = [], {}

    def __call__(self, method, *args, w=(), s=None, **kw):
        need = {}
        stack = [w]
        while stack:
            one = stack.pop()
            if one is None:
                continue
            if isinstance(one, tuple) and len(one) == 2 and isinstance(one[0], Sig):
                if self.seen.get(one[0], 0) < one[1]:
                    self.seen[one[0]] = need[one[0]] = one[1]
            else:
                stack.extend(one)
        self.ops.append((list(need.items()), method, args, kw, s))
        if s is None:
            return None
        s.n += s.step
        return s.now()

    def run(self, eng):
        for need, method, args, kw, s in self.ops:
            for sig, v in need:
                eng.wait_ge(sig.sem, v)
            ins = method(*args, **kw)
            if s is not None:
                ins.then_inc(s.sem, s.step)


class Bank:

    def __init__(self, ap):
        self.ap, self.free = ap, []


class Ring:
    def __init__(self, banks):
        self.banks, self.n = banks, 0

    def next(self):
        self.n += 1
        return self.banks[(self.n - 1) % len(self.banks)]


def program(nc, x, meta, wall, wf, bf, poolw, pscale, ng, fng, cvec, bada, gn1, gn2, gqk, rel, out):
    units = plan()
    crows = nc.dram_tensor("c_rows", (8, TOK), F32, kind="Internal").ap()
    kept = nc.dram_tensor("x_kept", (4, 128, D), F32, kind="Internal").ap()
    A, V, G, T, SY = nc.scalar, nc.vector, nc.gpsimd, nc.tensor, nc.sync

    with ExitStack() as ctx:
        def sb(name, shape, dt=F32, where=ctx):
            return where.enter_context(nc.sbuf_tensor(name, shape, dt))

        sigs = {}

        def S(name, step=1):
            if name not in sigs:
                sigs[name] = Sig(ctx.enter_context(nc.semaphore("s_" + name)), step)
            return sigs[name]

        def DS(name):
            return S(name, 16)

        pe, act, dve, pool, sp = Lane(), Lane(), Lane(), Lane(), Lane()

        psum = ctx.enter_context(nc.psum_tensor("psum", [128, 8, 512], F32))
        banks = [Bank(psum[:, i, :]) for i in range(8)]

        NR, NH = 3, 2
        raw = sb("raw", [128, NR, UNIT])
        wh = sb("wh", [128, NH, UNIT], F32R)
        wl = sb("wl", [128, NH, UNIT], F32R)
        hh = sb("hh", [128, 8, TOK], F32R)
        hl = sb("hl", [128, 8, TOK], F32R)
        ah = sb("ah", [128, 8, SEQ], F32R)
        al = sb("al", [128, 8, SEQ], F32R)
        ident = sb("ident", [128, 128])
        ones = sb("ones", [128, TOK])
        blk = sb("blk", [128, 2])
        mis = sb("mis", [128, 2112])
        gt = sb("gt", [128, 2, D])
        sgt = sb("sgt", [128, 2056])
        two = sb("two", [128, 2, SEQ])
        tmp = sb("tmp", [128, 2, SEQ])
        cols = sb("cols", [128, 4, 8])
        prm = sb("prm", [128, 56])
        cact = sb("cact", [128, 8])
        half = sb("half", [128, 16])
        sm = sb("sm", [128, 512])
        ccol = sb("ccol", [128, 4, 8])
        acc = mis[:, 0:2048]
        c_ng, c_ps, c_g1, c_g2, c_c, c_gqk, c_bf = (prm[:, 0:8], prm[:, 8:12], prm[:, 12:20], prm[:, 20:28],
                                                    prm[:, 28:36], prm[:, 36:38], prm[:, 38:39])
        for dst, src in ((c_ng, ng), (c_ps, pscale), (c_g1, gn1), (c_g2, gn2), (c_c, cvec), (c_gqk, gqk),
                         (c_bf, bf)):
            t_small = act(A.dma_start, dst, src, s=DS("d_small"))

        pool(G.memset, ones[:, :], 1.0, s=S("p_const"))
        pool(G.memset, half[:, :], -0.5, s=S("p_const"))
        t = pool(G.memset, ident[:, :], 0.0, s=S("p_const"))
        pool(G.affine_select, out=ident[:, :], in_=ident[:, :], compare_op=ALU.not_equal, fill=1.0, base=0,
             pattern=[[-1, 128]], channel_multiplier=1, w=t, s=S("p_const"))
        t = pool(G.memset, blk[:, :], 0.0, s=S("p_const"))
        pool(G.memset, blk[0:64, 0:1], 1.0, w=t, s=S("p_const"))
        t_const = pool(G.memset, blk[64:128, 1:2], 1.0, w=t, s=S("p_const"))

        st = {"dma": 0, "split": 0, "w": 0, "use": 0, "rate": 0, "due": 0, "ring": None,
              "last": sum(u[0] != "ada" for u in units) - 1}
        bg = []
        landed, slot_free, parts_of, done, ada = {}, {}, {}, {}, {"free": None}

        def load():
            n = st["dma"]
            if n < len(units):
                st["dma"] += 1
                landed[n] = sp(SY.dma_start, raw[:, n % NR, :], wall[n], w=slot_free.get(n - NR),
                               s=DS(f"d_w{n % NR}"))

        def ada_unit(n):
            _, _, kt, g = units[n]

            def clear():
                ada_finish()
                t0 = pool(G.memset, acc, 0.0, w=ada["free"], s=S("p_acc"))
                ada["t"] = [sp(SY.dma_start, acc[0:1, :], bada[g:g + 1, :], w=t0, s=DS("d_bada"))] * 4

            def piece(i):
                def run():
                    c = slice(512 * i, 512 * i + 512)
                    ada["t"][i] = dve(V.scalar_tensor_tensor, acc[:, c], raw[:, n % NR, c], cact[:, kt:kt + 1],
                                      acc[:, c], ALU.mult, ALU.add, w=[landed[n], ada["t"][i], t_cact],
                                      s=S("v_acc"))
                    if i == 3:
                        slot_free[n] = ada["t"][3]
                        load()
                        if kt == 7:
                            ada["ready"] = (g, ada["t"][3])
                return run

            if kt == 0:
                bg.append(clear)
            bg.extend(piece(i) for i in range(4))

        def split_next():
            while st["split"] < len(units) and units[st["split"]][0] == "ada":
                st["split"] += 1
                ada_unit(st["split"] - 1)
            n = st["split"]
            if n >= len(units):
                return
            st["split"] += 1
            w = st["w"]
            st["w"] += 1
            i, parts = w % NH, parts_of.setdefault(w, [])

            def piece(j):
                def run():
                    old = done.get(w - NH)
                    c = slice(512 * j, 512 * j + 512)
                    r = raw[:, n % NR, c]
                    t1 = act(A.activation, wh[:, i, c], r, ACT.Copy, w=[landed[n], old], s=S("a_wh"))
                    t2 = dve(V.tensor_tensor, wl[:, i, c], r, wh[:, i, c].bitcast(F32), ALU.subtract, w=[t1, old],
                             s=S("v_wl"))
                    parts.append([t1, t2])
                    if j == 3:
                        slot_free[n] = [t1, t2]
                        load()
                return run

            bg.extend(piece(j) for j in range(4))

        mod_tok = {}

        def ada_finish():
            if "ready" not in ada:
                return
            ring = st["ring"]
            g, tk = ada.pop("ready")
            ends = []
            for hf in range(2):
                which = 2 * g + hf
                if which in (2, 5):
                    row = gt[:, which // 3, :]
                    for c in range(2):
                        b = ring.next()
                        t = pe(T.matmul, b.ap, ones[:, 0:128], acc[:, 1024 * hf + 512 * c:1024 * hf + 512 * c + 512],
                               start=True, stop=True, w=[tk, b.free, t_const], s=S("t_ada"))
                        t2 = act(A.activation, row[:, 512 * c:512 * c + 512], b.ap, ACT.Copy,
                                 w=[t, st["za"]], s=S("a_ada"))
                        b.free = [t2]
                else:
                    b = ring.next()
                    for c in range(8):
                        o = 1024 * hf + 128 * c
                        t = pe(T.matmul, b.ap[:, 2 * c:2 * c + 2], acc[:, o:o + 128], ones[:, 0:2], start=(c == 0),
                               stop=(c == 7), skip_group_check=True, w=[tk, b.free, t_const], s=S("t_ada"))
                    j = {0: 0, 1: 1, 3: 2, 4: 3}[which]
                    src = b.ap[:, 0:16].rearrange("p (a b) -> p a b", b=2)[:, :, 0]
                    if which in (0, 3):
                        t2 = dve(V.tensor_copy, cols[:, j, :], src, w=t, s=S("v_ada"))
                    else:
                        t2 = dve(V.scalar_tensor_tensor, cols[:, j, :], src, 1.0, c_g1 if which == 1 else c_g2,
                                 ALU.add, ALU.mult, w=[t, t_small], s=S("v_ada"))
                    b.free = [t2]
                ends.append(t)
                mod_tok[which] = t2
            ada["free"] = ends

        queue = []

        def pump(left):
            for _ in range(-(-len(bg) // max(left, 1))):
                bg.pop(0)()

        def fill(n):
            st["due"] += n
            while st["due"] >= 1:
                st["due"] -= 1
                if queue:
                    queue.pop(0)()

        def drain():
            while queue:
                queue.pop(0)()

        class Unit:

            def __init__(self):
                w = self.w = st["use"]
                st["use"] += 1
                self.h, self.l = wh[:, w % NH, :], wl[:, w % NH, :]
                pump(1)
                while st["w"] <= w:
                    split_next()
                    pump(1)
                if w < st["last"]:
                    split_next()
                self.t, self.left = parts_of[w], 8

            def slot(self):
                if self.left:
                    pump(self.left)
                    self.left -= 1
                if self.left == 4:
                    ada_finish()

            def over(self, t):
                done[self.w] = t
                pump(1)

        def three(bank, lh, ll, rh, rl, first, last, w=None, s=None):
            pe(T.matmul, bank, lh, rh, start=first, stop=False, skip_group_check=True, w=w)
            pe(T.matmul, bank, lh, rl, start=False, stop=False, skip_group_check=True)
            return pe(T.matmul, bank, ll, rh, start=False, stop=last, skip_group_check=True, s=s)

        def group_cols(u, bank, src, src_tok, sub=0, base=None, nk=8, c0=0, n=SEQ, k0=0):
            for k in range(nk):
                o = (k * 256 + sub * 128) if base is None else base + 128 * k
                t = three(bank.ap[:, 0:n], u.h[:, o:o + 128], u.l[:, o:o + 128], src[0][:, k0 + k, c0:c0 + n],
                          src[1][:, k0 + k, c0:c0 + n], k == 0, k == nk - 1,
                          w=[src_tok[k0 + k], u.t[o // 512], bank.free if k == 0 else None],
                          s=S("t_mm") if k == nk - 1 else None)
                if n == SEQ:
                    if k % 2:
                        u.slot()
                    fill(st["rate"])
            return t

        def group_rows(src, src_tok, tiles, bank_of, evac, khs=(0, 1), before=None, mid=None):
            for kh in khs:
                if mid and kh == khs[1]:
                    mid()
                u = Unit()
                outer = before is not None and kh == khs[0]
                n = len(tiles)
                for i, k in ([(i, k) for k in range(4) for i in range(n)] if outer
                             else [(i, k) for i in range(n) for k in range(4)]):
                    c0, b = tiles[i], bank_of[i]
                    kk = 4 * kh + k
                    if before and i == 0:
                        before(kk)
                    t = three(b.ap, src[0][:, kk, c0:c0 + 128], src[1][:, kk, c0:c0 + 128],
                              u.h[:, 512 * k:512 * k + 512], u.l[:, 512 * k:512 * k + 512],
                              kh == khs[0] and k == 0, kh == khs[1] and k == 3,
                              w=[src_tok[kk], u.t[k], b.free if kh == khs[0] and k == 0 else None],
                              s=S("t_mm") if k == 3 else None)
                    if k % 2:
                        u.slot()
                    if k == 3 and kh == khs[1]:
                        evac(i, b, t)
                    fill(st["rate"])
                u.over(t)
            return t

        def split_sb(hi, lo, src, w):
            t1 = act(A.activation, hi, src, ACT.Copy, w=w, s=S("a_hi"))
            return [t1, dve(V.tensor_tensor, lo, src, hi.bitcast(F32), ALU.subtract, w=[t1, w], s=S("v_lo"))]

        def rstd(w, i, n, inv, rows=128):
            v = sm[0:rows, i:i + n]
            t = pool(G.tensor_scalar, v, v, inv, EPS, ALU.mult, ALU.add, w=w, s=S("p_ms"))
            return pool(G.tensor_tensor, v, v, half[0:rows, 0:n], ALU.pow, w=[t, t_const], s=S("p_rstd"))

        def square_sum(src, i, w, rows=128):
            j = tmp[0:rows, :, :].rearrange("p a b -> p (a b)")
            return act(A.activation, j, src, ACT.Square, accum_out=sm[0:rows, i:i + 1],
                       w=[w, S("a_sq").now(), S("v_tmp").now()], s=S("a_sq"))

        def transposed(tiles, ring, take):
            toks = {}

            def one(kt):
                b = ring.next()
                for i, (src, tk) in enumerate(tiles):
                    t = pe(T.transpose, b.ap[:, 128 * i:128 * i + 128], src[:, 128 * kt:128 * kt + 128],
                           ident[:, :], w=[tk, t_const, b.free if i == 0 else None],
                           s=S("t_tp") if i == len(tiles) - 1 else None)
                toks[kt] = take(kt, b, t)

            def ahead(kt):
                while len(toks) < min(8, kt + 4):
                    one(len(toks))
            return toks, ahead

        first = ExitStack()
        xt = sb("xt", [128, 4, D], where=first)
        xm = sb("xm", [META, D], where=first)
        wfb = sb("wfb", [128, 8, 128], where=first)
        wfh = sb("wfh", [128, 8, 128], F32R, where=first)
        wfl = sb("wfl", [128, 8, 128], F32R, where=first)
        fa, fe, fc = (sgt[:, TOK * i:TOK * i + TOK] for i in range(3))
        t_m = act(A.dma_start, xm[:, :], meta, s=DS("d_xm"))
        t_x = [sp(SY.dma_start, xt[:, i, :], x[128 * i:128 * i + 128, :], s=DS(f"d_x{i}")) for i in range(4)]
        t_wf = act(A.dma_start, wfb[:, :, :], wf, s=DS("d_wf"))
        for _ in range(NR):
            load()

        t = act(A.activation, sm[:, 300:308], c_c, ACT.Sigmoid, w=t_small, s=S("a_c"))
        t_cact = dve(V.tensor_tensor, cact[:, :], c_c, sm[:, 300:308], ALU.mult, w=[t, t_small], s=S("v_c"))

        normed = []
        for i, (src, tk, rows) in enumerate([(xm[:, :], t_m, META)] + [(xt[:, i, :], t_x[i], 128) for i in range(4)]):
            t = square_sum(src, 310 + i, tk, rows)
            r = rstd(t, 310 + i, 1, 1.0 / D, rows)
            t2 = dve(V.tensor_scalar, src, src, sm[0:rows, 310 + i:311 + i], None, ALU.mult, w=r, s=S("v_xn"))
            normed.append((src, t2))
        bm = banks[4]
        for kt in range(8):
            t = pe(T.transpose, bm.ap[:, 16 * kt:16 * kt + 16], xm[:, 128 * kt:128 * kt + 128],
                   ident[0:META, 0:META], w=[normed[0][1], t_const], s=S("t_tp"))
        for kt in range(8):
            t1 = act(A.activation, hh[:, kt, 0:META], bm.ap[:, 16 * kt:16 * kt + 16], ACT.Copy,
                     scale=c_ng[:, kt:kt + 1], w=[t, t_small], s=S("a_hi"))
        for kt in range(8):
            t_hm = dve(V.scalar_tensor_tensor, hl[:, kt, 0:META], bm.ap[:, 16 * kt:16 * kt + 16],
                       c_ng[:, kt:kt + 1], hh[:, kt, 0:META].bitcast(F32), ALU.mult, ALU.subtract, w=[t1, t],
                       s=S("v_lo"))
        bm.free = [t1, t_hm]

        def take_first(kt, b, t):
            g, o = c_ng[:, kt:kt + 1], hh[:, kt, META:TOK]
            t1 = act(A.activation, o, b.ap, ACT.Copy, scale=g, w=t, s=S("a_hi"))
            t2 = dve(V.scalar_tensor_tensor, hl[:, kt, META:TOK], b.ap, g, o.bitcast(F32), ALU.mult,
                     ALU.subtract, w=[t1, t], s=S("v_lo"))
            b.free = [t1, t2]
            return [t1, t2, t_hm]

        h_tok, ahead = transposed(normed[1:], Ring([banks[5], banks[6], banks[4]]), take_first)
        hs = (hh, hl)
        tw = split_sb(wfh[:, :, :], wfl[:, :, :], wfb[:, :, :], t_wf)

        at_tok, at_free = {}, [None]

        class Att:

            def __init__(self, kind, m, v2, p_sb, pt, tring, oring, sring, ybase, after=None):
                self.kind, self.m, self.v2, self.p, self.pt = kind, m, v2, p_sb, pt
                self.tring, self.oring, self.sring, self.ybase = tring, oring, sring, ybase
                self.off = [sum(m + 128 * (j + 1) for j in range(i)) for i in range(4)]
                self.ptoff = {0: 0, 1: 512, 2: 896, 3: 1152, -1: 1280}
                self.qk, self.extra, self.za = {}, {}, {}
                self.tok, self.used = {}, {}
                self.h0 = after.h0 + 8 if after else 0
                self.pused, self.ptt, self.ptused, self.o = ((after.pused, after.ptt, after.ptused, after.o) if after
                                                             else ({}, {}, {}, {}))
                self.vfree, self.vtok, self.pfree = None, None, None
                self.pair_over = {}
                self.prepare, self.begun = None, set()

            def score(self, h, i):
                m, kind, n = self.m, self.kind, 128 * (i + 1)
                if i == 3 and h < 7 and self.prepare:
                    self.prepare(h + 1)
                par = 64 * (h % 2)
                self.begun.add(4 * h + i)
                q, k, km, ready = self.qk[h // 2]
                ql = q[par:par + 64, 128 * i:128 * i + 128]
                P = self.p[:, h % 2, self.off[i]:self.off[i] + m + n]
                b = self.sring.next()
                over = [b]
                if m:
                    if n == 512:
                        over, both = [banks[4], banks[5]], psum[:, 4:6, :].rearrange("p a b -> p (a b)")
                        mb, sc, rb = both[:, 512 - m:512], both[:, 512 - m:512 + n], both[:, 512:512 + n]
                    else:
                        mb, sc, rb = b.ap[:, 0:m], b.ap[:, 0:m + n], b.ap[:, m:m + n]
                    pe(T.matmul, mb, ql, km[par:par + 64, :], start=True, stop=True, skip_group_check=True,
                       w=[ready, [o.free for o in over]])
                else:
                    sc = rb = b.ap[:, 0:n]
                t = pe(T.matmul, rb, ql, k[par:par + 64, 0:n], start=True, stop=True, skip_group_check=True,
                       w=[ready, [o.free for o in over]], s=S("t_sc"))
                self.pair_over[h // 2] = t
                old_p = [self.pused.get(self.h0 + h - 2), self.pfree]
                c = 320 + 4 * ((4 * h + i) % 16)
                mx, su, nmx = sm[:, c:c + 1], sm[:, c + 1:c + 2], sm[:, c + 2:c + 3]
                old = self.tok.get(4 * h + i - 16)
                diag = P[:, m + n - 128:m + n]
                if kind == "sb":
                    g = self.extra[(4 * h + i) % 2]
                    gg = g["ap"][:, 512 - n:512]
                    t1 = act(A.activation, P, sc, ACT.Sigmoid, w=[t, old_p], s=S("a_s"))
                    t1b = act(A.activation, gg, sc, ACT.Sigmoid, scale=-1.0, w=g["free"], s=S("a_s"))
                    b.free = [t1b]
                    t2a = pool(G.affine_select, out=diag, in_=diag, compare_op=ALU.is_gt, fill=0.0, base=0,
                               pattern=[[-1, 128]], channel_multiplier=1, w=t1, s=S("p_s"))
                    gd = g["ap"][:, 384:512]
                    t2 = pool(G.affine_select, out=gd, in_=gd, compare_op=ALU.is_gt, fill=1.0, base=0,
                              pattern=[[-1, 128]], channel_multiplier=1, w=t1b, s=S("p_s"))
                    yield
                    t3 = dve(V.tensor_tensor_scan, gg[:, ::-1], gg[:, ::-1], ones[:, 0:n], 1.0, ALU.mult, ALU.mult,
                             w=[t2, t1b, t_const], s=S("v_s"))
                    yield
                    t4 = dve(V.tensor_tensor, P, P, g["ap"][:, 513 - n:513], ALU.mult, w=[t3, t2, g["one"]],
                             s=S("v_p"))
                    g["free"] = [t4]
                    self.tok[4 * h + i] = t4
                    return
                if kind == "fg":
                    cb, cbt = self.extra[h]
                    t1 = dve(V.scalar_tensor_tensor, P, sc, ccol[:, i, h:h + 1], cb[:, 0:m + n], ALU.add,
                             ALU.subtract, w=[t, old_p, cbt, t_cc], s=S("v_s"))
                    for o in over:
                        o.free = [t1]
                    self.used[h] = t1
                    t2 = pool(G.affine_select, out=diag, in_=diag, compare_op=ALU.is_ge, fill=NEG, base=0,
                              pattern=[[-1, 128]], channel_multiplier=1, w=t1, s=S("p_s"))
                    yield
                    t3 = dve(V.tensor_reduce, nmx, P, AX.X, ALU.max, negate=True, w=[t2, old], s=S("v_m"))
                else:
                    bt, btt = self.extra[h]
                    t1 = dve(V.tensor_tensor_reduce, out=P, in0=sc, in1=bt[:, 512 - n:512], scale=1.0,
                             scalar=-3.0e38, op0=ALU.add, op1=ALU.max, accum_out=mx, w=[t, old_p, btt, old],
                             s=S("v_s"))
                    b.free = [t1]
                    self.used[h] = t1
                    yield
                    t3 = dve(V.tensor_scalar, nmx, mx, -1.0, None, ALU.mult, w=t1, s=S("v_m"))
                t4 = act(A.activation, P, P, ACT.Exp, bias=nmx, accum_out=su, w=[t3, t1, t2 if m else None],
                         s=S("a_s"))
                yield
                t5 = dve(V.reciprocal, mx, su, w=t4, s=S("v_m"))
                self.tok[4 * h + i] = act(A.activation, P, P, ACT.Copy, scale=mx, w=[t5, t4], s=S("a_p"))

            def turn(self, h, j):
                b = self.tring.next()
                i0, rows, w = max(j, 0), (128 if j >= 0 else META), 512 - 128 * max(j, 0)
                for i in range(i0, 4):
                    o = self.off[i] + (self.m + 128 * j if j >= 0 else 0)
                    t = pe(T.transpose, b.ap[:, 128 * (i - i0):128 * (i - i0) + 128], self.p[:, h % 2, o:o + 128],
                           ident[:, :], w=[self.tok[4 * h + i], b.free if i == i0 else None],
                           s=S("t_tp") if i == 3 else None)
                if j == 3:
                    self.pused[self.h0 + h] = t
                o = self.ptoff[j]
                ph, pl = self.pt
                old = [self.ptused.get(j), self.pfree]
                t1 = act(A.activation, ph[0:rows, o:o + w], b.ap[0:rows, 0:w], ACT.Copy, w=[t, old], s=S("a_pt"))
                t2 = dve(V.tensor_tensor, pl[0:rows, o:o + w], b.ap[0:rows, 0:w], ph[0:rows, o:o + w].bitcast(F32),
                         ALU.subtract, w=[t1, t, old], s=S("v_pt"))
                b.free = [t1, t2]
                self.ptt[j] = [t1, t2]

            def value(self, h, j):
                i0, rows, w, o = max(j, 0), (128 if j >= 0 else META), 512 - 128 * max(j, 0), self.ptoff[j]
                ph, pl = self.pt
                lhs = self.v2[0:rows, (j if j >= 0 else 4), h, :]
                start = (j == -1) if self.m else (j == 0)
                if start:
                    self.o["bank"] = self.oring.next()
                b = self.o["bank"]
                pe(T.matmul, b.ap[:, 128 * i0:512], lhs, ph[0:rows, o:o + w], start=start, stop=False,
                   skip_group_check=True, w=[self.ptt[j], self.vtok, b.free if start else None])
                t = pe(T.matmul, b.ap[:, 128 * i0:512], lhs, pl[0:rows, o:o + w], start=False, stop=(j == 3),
                       skip_group_check=True, s=S("t_pv"))
                self.ptused[j] = t
                if j == 3:
                    par = 64 * (h % 2)
                    t1 = act(A.activation, tmp[0:64, 0, :], b.ap[64:128, :], ACT.Copy,
                             w=[t, S("v_tmp").now(), S("a_sq").now()], s=S("a_o"))
                    t2 = dve(V.tensor_tensor, tmp[par:par + 64, 1, :], b.ap[0:64, :], tmp[0:64, 0, :], ALU.add,
                             w=[t1, t, self.o.get(0)], s=S("v_tmp"))
                    b.free = [t1, t2]
                    if par:
                        o = tmp[:, 1, :]
                        if self.kind == "fg":
                            z, zt = self.za[h // 2]
                            t2 = dve(V.tensor_tensor, o, o, z, ALU.mult, w=[t2, zt], s=S("v_tmp"))
                        p = self.ybase + h // 2
                        self.o[0] = at_tok[p] = split_sb(ah[:, p, :], al[:, p, :], o, [t2, at_free[0]])

        pend, lag, last_head = [], [], []

        def flush():
            for one in list(pend):
                if next(one[1], True):
                    pend.remove(one)

        def do_score(att, h, i):
            def run():
                flush()
                g = att.score(h, i)
                next(g)
                pend.append((att, g))
            return run

        def do_turn(att, h, j):
            def run():
                flush()
                while any(4 * h + i not in att.tok for i in range(4)):
                    flush()
                att.turn(h, j)
            return run

        def do_value():
            def run():
                flush()
                att, h, j = lag.pop(0)
                att.value(h, j)
            return run

        def push_head(att, h):
            scores = [do_score(att, h, i) for i in (3, 2, 1, 0)] if att else []
            if last_head:
                a, ph = last_head.pop()
                for r, j in enumerate(([-1] if a.m else []) + [0, 1, 2, 3]):
                    queue.append(do_turn(a, ph, j))
                    queue.append(lambda x=(a, ph, j): lag.append(x) or (len(lag) > 2 and do_value()()))
                    if scores:
                        queue.append(scores.pop(0))
            queue.extend(scores)
            if att:
                last_head.append((att, h))
            else:
                queue.extend([lambda: lag and do_value()()] * 2)

        def push_pair(att, p):
            push_head(att, 2 * p)
            push_head(att, 2 * p + 1)

        def scored(att, p):
            while p >= 0 and any(4 * h + i not in att.begun for h in (2 * p, 2 * p + 1) for i in range(4)):
                queue.pop(0)()

        def value_parts(att, rows_of):
            def evac(i, b, t):
                r = rows_of[i]
                src = b.ap[0:r, :].rearrange("p (h c) -> p h c", h=8)
                hi, lo = att.v2[0:r, i, :, 0:64], att.v2[0:r, i, :, 64:128]
                t1 = act(A.activation, hi, src, ACT.Copy, w=[t, att.vfree()], s=S("a_hi"))
                t2 = dve(V.tensor_tensor, lo, src, hi.bitcast(F32), ALU.subtract, w=[t1, t, att.vfree()],
                         s=S("v_lo"))
                b.free = [t1, t2]
                att.vtok = [t1, t2]
            return evac

        ub, us, pw = mis[:, 0:528], (mis[:, 528:1056], mis[:, 1056:1584]), mis[:, 1584:2096]
        za = gt.rearrange("p a b -> p (a b)").rearrange("p (a b) -> p a b", a=4)
        zp = two
        t_pw = act(A.dma_start, pw, poolw, s=DS("d_pw"))
        first.close()

        b1 = ExitStack()
        v2 = sb("v2", [128, 5, 8, 128], F32R, where=b1)
        p_sb = sb("p_sb", [128, 2, 4 * META + 1280], where=b1)
        pth = sb("pth", [128, 1280 + SEQ], F32R, where=b1)
        ptl = sb("ptl", [128, 1280 + SEQ], F32R, where=b1)
        q_sb = sb("q_sb", [128, 2, SEQ], where=b1)
        k_sb = sb("k_sb", [128, 2, SEQ], where=b1)
        km_sb = sb("km_sb", [128, 2, META], where=b1)
        cb = sb("cb", [128, 2, TOK], where=b1)

        tring = Ring([banks[3], banks[6]])
        fg = Att("fg", META, v2, p_sb, (pth, ptl), tring, Ring([banks[2], banks[7]]), Ring([banks[4], banks[5]]), 4)
        fg.vfree = lambda: S("t_tp").now()

        def row_of_c(h):
            i = h % 2
            fg.extra[h] = (cb[:, i, :], sp(SY.dma_start, cb[:, i, :], crows[h:h + 1, :].to_broadcast([128, TOK]),
                                           w=[t_crow, first_over, fg.used.get(h - 2)], s=DS(f"d_cb{i}")))
        fg.prepare = row_of_c

        group_rows(hs, h_tok, [META, META + 128, META + 256, META + 384, 0], banks[0:4] + [banks[7]],
                   value_parts(fg, [128, 128, 128, 128, META]), before=ahead)
        pr = Ring(banks[0:2])

        fb, fmb = banks[5], banks[6]
        for (b, c0, n) in ((fmb, 0, META), (fb, META, SEQ)):
            for k in range(8):
                t = three(b.ap[:, 0:n], wfh[:, k, :], wfl[:, k, :], hh[:, k, c0:c0 + n], hl[:, k, c0:c0 + n],
                          k == 0, k == 7, w=[tw, h_tok[k], b.free], s=S("t_mm") if k == 7 else None)
        dve(V.tensor_scalar, fa[:, 0:META], fmb.ap[:, 0:META], c_bf, None, ALU.add, w=[t, t_small], s=S("v_f"))
        ta = dve(V.tensor_scalar, fa[:, META:TOK], fb.ap, c_bf, None, ALU.add, w=t, s=S("v_f"))
        fb.free, fmb.free = [ta], [ta]
        tb = act(A.activation, fe[:, :], fa[:, :], ACT.Abs, w=ta, s=S("a_f"))
        tb = act(A.activation, fe[:, :], fe[:, :], ACT.Exp, scale=-1.0, w=tb, s=S("a_f"))
        tb = act(A.activation, fe[:, :], fe[:, :], ACT.Ln, bias=1.0, w=tb, s=S("a_f"))
        ta = dve(V.scalar_tensor_tensor, fa[:, :], fa[:, :], 0.0, fe[:, :], ALU.min, ALU.subtract, w=[ta, tb],
                 s=S("v_f"))
        ta = dve(V.tensor_tensor_scan, fc[:, :], ones[:, :], fa[:, :], 0.0, ALU.mult, ALU.add, w=[ta, t_const],
                 s=S("v_f"))
        t_crow = sp(SY.dma_start, crows, fc[0:8, :], w=ta, s=DS("d_c"))
        first_over = [S("t_tp").now(), S("t_mm").now()]
        fg.pfree = first_over
        row_of_c(0)

        def columns_of_c():
            for i in range(4):
                t = pe(T.transpose, fb.ap[:, 128 * i:128 * i + 128], fc[:, META + 128 * i:META + 128 * i + 128],
                       ident[:, :], w=[ta, fb.free], s=S("t_tp"))
            t2 = dve(V.tensor_copy, ccol[:, :, :], fb.ap.rearrange("p (i c) -> p i c", i=4)[:, :, 0:8], w=t,
                     s=S("v_cc"))
            fb.free = [t2]
            return t, t2

        def gate(dst, b, t, w):
            t1 = act(A.activation, dst, b.ap, ACT.Sigmoid, w=[t, w], s=S("a_z"))
            t2 = dve(V.tensor_tensor, dst, b.ap, dst, ALU.mult, w=[t1, t], s=S("v_z"))
            b.free = [t1, t2]
            return t2

        for j in range(2):
            u = Unit()
            for sub in range(2):
                b = pr.next()
                t = group_cols(u, b, hs, h_tok, sub, c0=META)
                fg.za[2 * j + sub] = (za[:, 2 * j + sub, :], gate(za[:, 2 * j + sub, :], b, t, None))
            u.over(t)
            if j == 0:
                t_cp, t_cc = columns_of_c()

        def meta_cols(u, sub, dst, w):
            b = tring.next()
            t = group_cols(u, b, hs, h_tok, sub, c0=0, n=META)
            b.free = [act(A.activation, dst, b.ap[:, 0:META], ACT.Copy, w=[t, w], s=S("a_m"))]
            return b.free[0], t

        st["rate"] = 1
        late = []

        def project_qk(p):
            i = p % 2
            u = Unit()
            scored(fg, p - 2)
            old = [fg.pair_over.get(p - 2), first_over]
            b = pr.next()
            t = group_cols(u, b, hs, h_tok, 0, c0=META)
            tq = act(A.activation, q_sb[:, i, :], b.ap, ACT.Copy, scale=0.125, w=[t, old], s=S("a_q"))
            b.free = [tq]
            b = pr.next()
            t = group_cols(u, b, hs, h_tok, 1, c0=META)
            tk = act(A.activation, k_sb[:, i, :], b.ap, ACT.Copy, w=[t, old], s=S("a_q"))
            b.free = [tk]
            tm, t = meta_cols(u, 1, km_sb[:, i, :], old)
            u.over(t)
            fg.qk[p] = (q_sb[:, i, :], k_sb[:, i, :], km_sb[:, i, :], [tq, tk, tm])
            push_pair(fg, p)

        def project_uz(p):
            i = p % 2
            u = Unit()
            b = pr.next()
            t = group_cols(u, b, hs, h_tok, 0, c0=META)
            if late:
                late.pop()()
            tu1 = act(A.activation, ub[:, META:TOK], b.ap, ACT.Copy, w=[t, used["ub"]], s=S("a_m"))
            b.free = [tu1]
            tu, t = meta_cols(u, 0, ub[:, 0:META], used["ub"])
            src, lo, tt = ub, 0, [tu, tu1, used["us"]]
            for s_ in range(p + 1):
                dst, dd = us[s_ % 2], 1 << s_
                lo += dd
                tt = dve(V.tensor_tensor, dst[:, lo:TOK], src[:, lo:TOK], src[:, lo - dd:TOK - dd], ALU.add,
                         w=tt, s=S("v_u"))
                src = dst
            pd = us[(p + 1) % 2][:, META:TOK]
            tt = dve(V.scalar_tensor_tensor, pd, src[:, META:TOK], 1.0 / (2 << p), ub[:, META:TOK], ALU.mult,
                     ALU.subtract, w=tt, s=S("v_u"))
            used["ub"] = tt
            b = pr.next()
            t = group_cols(u, b, hs, h_tok, 1, c0=META)
            u.over(t)
            yo = zp[:, i, :]
            tz = gate(yo, b, t, used.get(("zp", p - 2)))

            def product():
                b = tring.next()
                t = pe(T.matmul, b.ap, pw[:, 128 * p:128 * p + 128], pd, start=True, stop=True,
                       w=[tt, t_pw, b.free], s=S("t_y"))
                used["us"] = t
                t3 = dve(V.scalar_tensor_tensor, yo, b.ap, c_ps[:, p:p + 1], yo, ALU.mult, ALU.mult, w=[t, tz],
                         s=S("v_y"))
                b.free = [t3]
                used["zp", p] = at_tok[p] = split_sb(ah[:, p, :], al[:, p, :], yo, t3)
            late.append(product)

        used = {"us": None, "ub": None}
        for kind, p in ORDER_1:
            if kind == "qk":
                project_qk(p)
            else:
                project_uz(p)
        push_head(None, None)
        late.pop()()
        ada["free"] = [used["us"], used["ub"]]

        sg = sgt[:, 0:2048].rearrange("p (a b) -> p a b", a=4)
        mt = two
        sg_used = {n: [t_crow, t_cp] for n in range(4)}
        mt_used, m_tok = used["zp", 3], {}
        for e_ in range(4):
            sgo = {}
            for dd in range(2):
                u = Unit()
                for sub in range(2):
                    b = pr.next()
                    t = group_cols(u, b, hs, h_tok, sub, c0=META)
                    n = 2 * dd + sub
                    sgo[n] = act(A.activation, sg[:, n, :], b.ap, ACT.Sigmoid, w=[t, sg_used.get(n)], s=S("a_g"))
                    b.free = [sgo[n]]
                u.over(t)
            if e_ == 0:
                drain()
                st["rate"] = 0
                b1.close()
                b1_over = [S("t_pv").now(), S("t_tp").now(), S("a_pt").now(), S("v_pt").now(), at_tok[7],
                           S("v_s").now()]
                st["za"] = at_tok[7]
                w1 = ExitStack()
                x1 = sb("x1", [128, 4, D], where=w1)
                gf = sb("gf", [128, D], where=w1)
                w1a = ExitStack()
                mh = sb("mh", [128, 8, SEQ], F32R, where=w1a)
                ml = sb("ml", [128, 8, SEQ], F32R, where=w1a)
                t_x1 = [sp(SY.dma_start, x1[:, i, :], x[128 * i:128 * i + 128, :], w=b1_over, s=DS(f"d_x{i}"))
                        for i in range(4)]
                t_gf = sp(SY.dma_start, gf[:, :], fng.to_broadcast([128, D]), w=b1_over, s=DS("d_gf"))
                st["ring"] = Ring([banks[3], banks[6]])
            u = Unit()
            for dd in range(2):
                n = 2 * e_ + dd
                b = pr.next()
                t = group_cols(u, b, (ah, al), at_tok, base=dd * 1024, nk=4)
                t1 = dve(V.tensor_tensor, mt[:, 0, :], b.ap, sg[:, 2 * dd, :], ALU.mult,
                         w=[t, sgo[2 * dd], mt_used], s=S("v_m1"))
                b.free = [t1]
                b = pr.next()
                t = group_cols(u, b, (ah, al), at_tok, base=dd * 1024 + 512, nk=4, k0=4)
                t2 = dve(V.tensor_tensor, mt[:, 1, :], b.ap, sg[:, 2 * dd + 1, :], ALU.mult,
                         w=[t, sgo[2 * dd + 1], mt_used], s=S("v_m1"))
                b.free = [t2]
                sg_used[2 * dd], sg_used[2 * dd + 1] = t1, t2
                t3 = dve(V.tensor_tensor, mt[:, 0, :], mt[:, 0, :], mt[:, 1, :], ALU.add, w=[t1, t2], s=S("v_m1"))
                mt_used = m_tok[n] = split_sb(mh[:, n, :], ml[:, n, :], mt[:, 0, :], [t3, b1_over])
            u.over(t)
        at_free[0] = t

        t1s, normed, chains, t_kept, m_over = {}, {}, [], [], []

        def tick():
            for g in list(chains):
                if next(g, True):
                    chains.remove(g)

        def both_norms(i):
            xi = x1[:, i, :]
            t = square_sum(xi, 384 + i, [t1s[i, 0], t1s[i, 1]])
            yield
            r = rstd(t, 384 + i, 1, 1.0 / D)
            yield
            t = dve(V.scalar_tensor_tensor, xi, xi, sm[:, 384 + i:385 + i], gf[:, :], ALU.mult, ALU.mult,
                    w=[r, t_gf, t1s[i, 1]], s=S("v_xn"))
            t_kept.append(sp(SY.dma_start, kept[i], xi, w=t, s=DS(f"d_k{i}")))
            yield
            t2 = square_sum(xi, 388 + i, t)
            yield
            r = rstd(t2, 388 + i, 1, 1.0 / D)
            yield
            t = dve(V.tensor_scalar, xn[:, i, :], xi, sm[:, 388 + i:389 + i], None, ALU.mult, w=[r, m_over[0], t],
                    s=S("v_xn"))
            normed[i] = (xn[:, i, :], t)

        def evac_out(ch):
            def evac(i, b, t):
                o = x1[:, i, 512 * ch:512 * ch + 512]
                t1s[i, ch] = dve(V.tensor_tensor, o, b.ap, o, ALU.add, w=[t, t_x1[i]], s=S("v_r"))
                b.free = [t1s[i, ch]]
                if ch:
                    tick()
                    chains.append(both_norms(i))
            return evac

        for ch in range(2):
            bk = banks[0:4] if ch == 0 else [banks[4], banks[5], banks[7], banks[3]]
            st["ring"] = Ring([banks[6]])
            t = group_rows((mh, ml), m_tok, [0, 128, 256, 384], bk, evac_out(ch))
        w1a.close()
        xn = sb("xn", [128, 4, D], where=w1)
        m_over.append(t)
        while chains:
            tick()

        def take_mod(j, old):
            def take(kt, b, t):
                o, d = kt % 2, two[:, kt % 2, :]
                t0 = dve(V.tensor_scalar, d, b.ap, cols[:, j + 1, kt:kt + 1], cols[:, j, kt:kt + 1], ALU.mult,
                         ALU.add, w=[t, mod_tok[{0: 0, 2: 3}[j]], mod_tok[{0: 1, 2: 4}[j]], two_used[o]],
                         s=S("v_two"))
                b.free = [t0]
                two_used[o] = split_sb(hh[:, kt, 0:SEQ], hl[:, kt, 0:SEQ], d, [t0, old])
                return two_used[o]
            return take

        two_used = [mt_used, mt_used]
        h_tok, ahead = transposed([normed[i] for i in range(4)], Ring(banks[0:4]), take_mod(0, m_over))
        w1.close()
        st["ring"] = Ring([banks[3]])

        b2 = ExitStack()
        v_ca = sb("v_ca", [128, 4, 8, 128], F32R, where=b2)
        v_sb = sb("v_sb", [128, 4, 8, 128], F32R, where=b2)
        p_sb = sb("p_sb2", [128, 2, 1280], where=b2)
        pth = sb("pth2", [128, 1280], F32R, where=b2)
        ptl = sb("ptl2", [128, 1280], F32R, where=b2)
        q_sb = sb("q_sb2", [128, 2, SEQ], where=b2)
        k_sb = sb("k_sb2", [128, 2, SEQ], where=b2)
        bt = (sgt[:, 0:512], sgt[:, 512:1024])
        gb = (sgt[:, 1024:1537], sgt[:, 1538:2051])
        sq = two

        pr = Ring(banks[0:2])
        tring, oring, sring = Ring([banks[3], banks[6]]), Ring([banks[2], banks[7]]), Ring([banks[4], banks[5]])
        ca = Att("ca", 0, v_ca, p_sb, (pth, ptl), tring, oring, sring, 4)
        sbk = Att("sb", 0, v_sb, p_sb, (pth, ptl), tring, oring, sring, 0, after=ca)

        def norm_over():
            return [t_kept, S("t_tp").now(), S("a_sq").now(), S("v_xn").now()]
        ca.vfree = norm_over

        def table(h):
            i = h % 2
            t = sp(SY.dma_start, bt[i], rel[h], w=[sg_used[0], sg_used[1], ca.used.get(h - 2)], s=DS(f"d_bt{i}"))
            ca.extra[h] = (bt[i], pool(G.memset, bt[i][0:64, 448:512], NEG, w=t, s=S("p_bt")))
        ca.prepare = table
        table(0)

        hs2 = (hh, hl)
        group_rows(hs2, h_tok, [0, 128, 256, 384], [banks[4], banks[5], banks[7], banks[6]],
                   value_parts(ca, [128] * 4), before=ahead)
        x1_over = norm_over()
        sbk.vfree = lambda: x1_over
        ca.pfree = sbk.pfree = x1_over
        st["rate"] = RATE_CA
        qs = [(q_sb[:, i, :], k_sb[:, i, :]) for i in range(2)] + [(mis[:, 1024:1536], mis[:, 1536:2048])]

        def place(g):
            if g >= 3:
                att, p = (ca, g - 3) if g < 7 else (sbk, g - 7)
                scored(att, p)
                return qs[g % 3], att.pair_over[p]
            return qs[g % 3], [x1_over, ada["free"]]

        def other_banks():
            mine = ca.o["bank"]
            bk = [banks[0], banks[1], banks[3], banks[2] if mine is banks[7] else banks[7]]
            return mine, bk
        one = [pool(G.memset, gb[i][:, 512:513], 1.0, w=[sg_used[2], sg_used[3]], s=S("p_bt")) for i in range(2)]
        sbk.extra = {i: {"ap": gb[i], "free": None, "one": one[i]} for i in range(2)}
        wide = mis[:, 0:1024].rearrange("p (c f) -> p c f", f=64)
        ss = {"sq": None, "wide": ada["free"]}

        def project_sb(p):
            u = Unit()
            qk, old = place(4 + p)
            got = []
            for sub in range(2):
                b = pr.next()
                t = group_cols(u, b, hs2, h_tok, sub)
                t1 = act(A.activation, qk[sub], b.ap, ACT.Copy, scale=(0.125, 1.0)[sub],
                         w=[t, old], s=S("a_q"))
                b.free = [t1]
                got.append(t1)
            u.over(t)
            sbk.qk[p] = (*qk, None, got)
            push_pair(sbk, p)

        def project_ca(p):
            u = Unit()
            qk, old = place(p)
            got, r = [], {}
            for sub in range(2):
                b = pr.next()
                t = group_cols(u, b, hs2, h_tok, sub)
                ts = act(A.activation, sq[:, sub, :], b.ap, ACT.Square, w=[t, two_used[sub], ss["sq"]],
                         s=S("a_sqk"))
                t1 = dve(V.tensor_scalar, qk[sub], b.ap, c_gqk[:, sub:sub + 1],
                         (0.125, 1.0)[sub], ALU.mult, ALU.mult, w=[t, ts, old, t_small], s=S("v_q"))
                b.free = [ts, t1]
                got.append((ts, t1))
            u.over(t)
            ca.qk[p] = [*qk, None, []]

            def sums():
                b = ca.tring.next()
                for sub in range(2):
                    for tt_ in range(4):
                        c = 8 * sub + 2 * tt_
                        t = pe(T.matmul, b.ap[:, c:c + 2], sq[:, sub, 128 * tt_:128 * tt_ + 128], blk[:, :],
                               start=(c == 0), stop=(c == 14), skip_group_check=True,
                               w=[got[sub][0], b.free, t_const], s=S("t_ss"))
                ss["sq"] = t
                t1 = dve(V.tensor_copy, sm[:, 400:416], b.ap[:, 0:16], w=[t, S("v_ss").now()], s=S("v_ss"))
                b.free = [t1]
                r["t"] = rstd(t1, 400, 16, 1.0 / 64)

            def widen():
                r["t"] = dve(V.tensor_copy, wide, sm[:, 400:416].unsqueeze(2).to_broadcast([128, 16, 64]),
                             w=[r["t"], ss["wide"]], s=S("v_ss"))

            def scale(sub):
                def run():
                    dst = qk[sub]
                    b = ca.tring.next()
                    for tt_ in range(4):
                        c = 64 * (8 * sub + 2 * tt_)
                        t = pe(T.matmul, b.ap[:, 128 * tt_:128 * tt_ + 128], mis[:, c:c + 128], ident[:, :],
                               start=(tt_ == 0), stop=(tt_ == 3), skip_group_check=True,
                               w=[r["t"], b.free, t_const], s=S("t_ss"))
                    t1 = dve(V.tensor_tensor, dst, dst, b.ap, ALU.mult, w=[t, got[sub][1]], s=S("v_q"))
                    b.free = [t1]
                    ca.qk[p][3].append(t1)
                    ss["wide"] = t
                return run

            for at, fn in ((2, sums), (14, widen), (18, scale(0)), (20, scale(1))):
                queue.extend([flush] * (at - len(queue)))
                queue.insert(at, fn)
            push_pair(ca, p)

        for p in range(4):
            project_ca(p)
        mine, bk = other_banks()
        ca.tring, ca.oring = Ring([banks[6]]), Ring([mine])
        group_rows(hs2, h_tok, [0, 128, 256, 384], bk, value_parts(sbk, [128] * 4))
        ca.tring, ca.oring = tring, oring
        st["rate"] = RATE_SB
        for p in range(4):
            project_sb(p)
        push_head(None, None)

        w2 = ExitStack()
        kp = {}

        def attention_over():
            drain()
            st["rate"] = 0
            b2.close()
            kp["over"] = [S("t_pv").now(), S("t_tp").now(), S("a_pt").now(), S("v_pt").now(), at_tok[3]]
            kp["x"], kp["xn"] = sb("x1b", [128, 4, D], where=w2), sb("xnb", [128, 4, D], where=w2)
            for i in range(4):
                t_x1[i] = sp(SY.dma_start, kp["x"][:, i, :], kept[i], w=[kp["over"], t_kept], s=DS(f"d_x{i}"))
            tmp_used.update({0: S("v_tmp").now(), 1: at_tok[3]})

        tmp_used, t_x1 = {}, {}
        res = {}

        def add_gated(j, ch):
            def evac(i, b, t):
                o = kp["x"][:, i, 512 * ch:512 * ch + 512]
                d = tmp[:, i % 2, :]
                t1 = dve(V.tensor_tensor, d, b.ap, gt[:, j, 512 * ch:512 * ch + 512], ALU.mult,
                         w=[t, mod_tok[{0: 2, 1: 5}[j]], tmp_used[i % 2], S("a_sq").now()], s=S("v_tmp"))
                b.free = [t1]
                res[i, ch] = tmp_used[i % 2] = dve(V.tensor_tensor, o, o, d, ALU.add,
                                                   w=[t1, t_x1[i], res.get((i, ch))], s=S("v_tmp"))
            return evac

        normed = {}

        def norm_again(i):
            xi = kp["x"][:, i, :]
            t = square_sum(xi, 420 + i, [res[i, 0], res[i, 1]])
            yield
            r = rstd(t, 420 + i, 1, 1.0 / D)
            yield
            t = dve(V.tensor_scalar, kp["xn"][:, i, :], xi, sm[:, 420 + i:421 + i], None, ALU.mult,
                    w=[r, kp["over"]], s=S("v_xn"))
            normed[i] = (kp["xn"][:, i, :], t)

        def evac_o(ch):
            add = add_gated(0, ch)

            def evac(i, b, t):
                add(i, b, t)
                if ch:
                    tick()
                    chains.append(norm_again(i))
            return evac

        mine, bk = other_banks()
        for a_ in (ca, sbk):
            a_.tring, a_.oring = Ring([banks[6]]), Ring([mine])
        tiles = [0, 128, 256, 384]
        st["rate"] = RATE_WO
        group_rows((ah, al), at_tok, tiles, bk, evac_o(0), (1, 0), mid=attention_over)
        t = group_rows((ah, al), at_tok, tiles, [banks[4], banks[5], banks[6], mine], evac_o(1), (1, 0))
        x1 = kp["x"]
        at_free[0] = t
        h_over = S("t_mm").now()
        while chains:
            tick()
        two_used = [ss["sq"], ss["sq"]]
        h_tok, ahead = transposed([normed[i] for i in range(4)], Ring(banks[0:4]), take_mod(2, h_over))

        r_sb = two
        tmp_used = {0: S("a_sq").now(), 1: S("a_sq").now()}
        pr = Ring(banks[0:4])
        r_used = [None, None]
        a_old = at_free[0]
        s2 = (sgt[:, 0:512], sgt[:, 512:1024])
        s_used = [[ca.used[6], ca.used[7]]] * 2
        t_out = []
        for q in range(4):
            for j in range(4):
                u = Unit()
                start = q == 0 and j == 0
                if start:
                    for k in range(8):
                        ahead(k)
                        for sub in range(2):
                            o = k * 256 + sub * 128
                            t = three(banks[4 + sub].ap, u.h[:, o:o + 128], u.l[:, o:o + 128], hs2[0][:, k, 0:SEQ],
                                      hs2[1][:, k, 0:SEQ], k == 0, k == 7,
                                      w=[h_tok[k], u.t[o // 512], banks[4 + sub].free if k == 0 else None],
                                      s=S("t_mm") if k == 7 else None)
                        u.slot()
                for sub in range(2):
                    n = 2 * j + sub
                    if start:
                        b = banks[4 + sub]
                    else:
                        b = pr.next()
                        t = group_cols(u, b, hs2, h_tok, sub)
                    t1 = act(A.activation, r_sb[:, sub, :], b.ap, ACT.Relu, w=[t, r_used[sub] or two_used[sub]], s=S("a_r"))
                    t2 = dve(V.scalar_tensor_tensor, s2[sub], b.ap, 0.0, r_sb[:, sub, :], ALU.max, ALU.mult,
                             w=[t1, t, s_used[sub]], s=S("v_r2"))
                    r_used[sub] = t2
                    b.free = [t1, t2]
                    s_used[sub] = at_tok[n] = split_sb(ah[:, n, :], al[:, n, :], s2[sub], [t2, a_old])
                u.over(t)
            for ch in range(2):
                bk = banks[4:8] if ch == 0 else banks[0:4]
                evac = add_gated(1, ch)

                def last(i, b, t, evac=evac, ch=ch):
                    evac(i, b, t)
                    t_out.append(act(A.dma_start, out[128 * i:128 * i + 128, 512 * ch:512 * ch + 512],
                                     x1[:, i, 512 * ch:512 * ch + 512], w=res[i, ch], s=DS("d_out")))
                t = group_rows((ah, al), at_tok, [0, 128, 256, 384], bk, last if q == 3 else evac)
            a_old = t
        w2.close()

        block = ctx.enter_context(nc.Block())

        @block.sync
        def _(eng):
            sp.run(eng)
            eng.wait_ge(t_crow[0].sem, t_crow[1])
            for s_, v in t_kept:
                eng.wait_ge(s_.sem, v)

        @block.scalar
        def _(eng):
            act.run(eng)
            eng.wait_ge(t_out[-1][0].sem, t_out[-1][1])

        @block.vector
        def _(eng):
            dve.run(eng)

        @block.gpsimd
        def _(eng):
            pool.run(eng)

        @block.tensor
        def _(eng):
            pe.run(eng)


def kernel(x, meta_tokens, norm_g, w_in, b_forget, pool_w, pool_scale, w_up_pool, w_up_attn, w_out, final_norm_g,
           c_2, g_norm1_2, w_in_2, g_q_2, g_k_2, rel_bias_2, w_o_2, g_norm2_2, w1_2, w2_2, w_ada_2, b_ada_2):
    import numpy as np
    import concourse.bacc as bacc
    from concourse.bass_utils import run_bass_kernel_spmd

    a = {n: np.asarray(v)[0] for n, v in dict(w_in=w_in, w_out=w_out, w_in_2=w_in_2, w_o_2=w_o_2, w1_2=w1_2,
                                              w2_2=w2_2, w_ada_2=w_ada_2, up=w_up_pool, ua=w_up_attn).items()}

    def columns(v):
        return np.ascontiguousarray(np.asarray(v).reshape(-1, 128).T)

    def packed(unit):
        kind, name, p, q = unit
        if kind == "cols":
            w = a[name]
            both = np.concatenate([w[:, p:p + 128], w[:, q:q + 128]], 1)
            return both.reshape(8, 128, 256).transpose(1, 0, 2).reshape(128, UNIT)
        if kind == "rows":
            return a[name][512 * p:512 * p + 512, q:q + 512].reshape(4, 128, 512).transpose(1, 0, 2).reshape(128, UNIT)
        if kind == "ada":
            return a[name][128 * p:128 * p + 128, UNIT * q:UNIT * q + UNIT]
        tiles = [a[s][:, 128 * d:128 * d + 128].reshape(4, 128, 128).transpose(1, 0, 2).reshape(128, 512)
                 for d in (2 * p, 2 * p + 1) for s in ("up", "ua")]
        return np.concatenate(tiles, 1)

    f = np.tile(a["w_in"][:, C_F:C_F + 8], (1, 16)).reshape(8, 128, 128).transpose(1, 0, 2)
    far = np.clip(384 + np.arange(128)[:, None] - np.arange(512)[None, :], -128, 128) + 128
    rel = np.asarray(rel_bias_2)[0][:, far]
    arrays = {
        "x": np.asarray(x)[0],
        "meta": np.asarray(meta_tokens),
        "wall": np.stack([packed(u) for u in plan()]),
        "wf": f,
        "bf": np.tile(np.asarray(b_forget)[0], 16).reshape(128, 1),
        "poolw": np.asarray(pool_w)[0].transpose(1, 0, 2).reshape(128, 512),
        "pscale": columns(np.asarray(pool_scale)[0]),
        "ng": columns(np.asarray(norm_g)[0]),
        "fng": np.asarray(final_norm_g).reshape(1, D),
        "cvec": columns(np.asarray(c_2)[0]),
        "bada": np.asarray(b_ada_2)[0].reshape(3, UNIT),
        "gn1": columns(np.asarray(g_norm1_2)[0]),
        "gn2": columns(np.asarray(g_norm2_2)[0]),
        "gqk": np.stack([np.tile(np.asarray(g_q_2)[0], 2), np.tile(np.asarray(g_k_2)[0], 2)], 1),
        "rel": rel,
    }
    arrays = {n: np.ascontiguousarray(v) for n, v in arrays.items()}
    nc = bacc.Bacc("TRN2", target_bir_lowering=False, num_devices=1, dynamic_dma_scratch_size=1024)
    args = [nc.dram_tensor("in_" + n, v.shape, mybir.dt.from_np(v.dtype), kind="ExternalInput").ap()
            for n, v in arrays.items()]
    out = nc.dram_tensor("out", (SEQ, D), F32, kind="ExternalOutput").ap()
    program(nc, *args, out)
    r = run_bass_kernel_spmd(nc, [{"in_" + n: v for n, v in arrays.items()}], core_ids=[0])
    return r.results[0]["out"].reshape(1, SEQ, D)
```

```python
from contextlib import ExitStack

import concourse.bass as bass
from concourse import mybir

F32 = mybir.dt.float32
F32R = mybir.dt.float32r
ALU = mybir.AluOpType
ACT = mybir.ActivationFunctionType
AX = mybir.AxisListType

D = 1024
SEQ = 512
META = 16
TOK = META + SEQ
UNIT = 2048
RATE_CA, RATE_SB, RATE_WO = 1.5, 2, 2.5
NEG = -1.0e30
EPS = 1e-6

C_U, C_ZP, C_Q, C_K, C_V, C_ZA, C_F, C_GP, C_GA = 0, 512, 1024, 1536, 2048, 2560, 3072, 3080, 4104


ORDER_1 = (("qk", 0), ("qk", 1), ("uz", 0), ("qk", 2), ("uz", 1), ("qk", 3), ("uz", 2), ("uz", 3))


def plan():
    ada = [("ada", "w_ada_2", kt, g) for g in range(3) for kt in range(8)]
    out = [("rows", "w_in", kh, C_V) for kh in range(2)]
    out += [("cols", "w_in", C_ZA + 256 * j, C_ZA + 256 * j + 128) for j in range(2)]
    for kind, p in ORDER_1:
        out.append(("cols", "w_in", (C_Q if kind == "qk" else C_U) + 128 * p, (C_K if kind == "qk" else C_ZP) + 128 * p))
    for e in range(4):
        n = (1, 2, 2) if e == 3 else (2, 1, 2)
        for i, d in enumerate((2 * e, 2 * e + 1)):
            out.append(("cols", "w_in", C_GP + 128 * d, C_GA + 128 * d))
            out += [ada.pop(0) for _ in range(n[i])]
        out.append(("up", "", e, 0))
        out += [ada.pop(0) for _ in range(n[2])]
    for ch in range(2):
        for kh in range(2):
            out.append(("rows", "w_out", kh, 512 * ch))
            out.append(ada.pop(0))
    out += [("rows", "w_in_2", kh, 2560) for kh in range(2)]
    for p in range(4):
        out.append(("cols", "w_in_2", 1536 + 128 * p, 2048 + 128 * p))
    out += [("rows", "w_in_2", kh, 1024) for kh in range(2)]
    for p in range(4):
        out.append(("cols", "w_in_2", 128 * p, 512 + 128 * p))
    for ch in range(2):
        for kh in (1, 0):
            out.append(("rows", "w_o_2", kh, 512 * ch))
    for q in range(4):
        for j in range(4):
            out.append(("cols", "w1_2", 1024 * q + 256 * j, 1024 * q + 256 * j + 128))
        for ch in range(2):
            for kh in range(2):
                out.append(("rows", "w2_2", 2 * q + kh, 512 * ch))
    assert not ada
    return out


class Sig:

    def __init__(self, sem, step):
        self.sem, self.step, self.n = sem, step, 0

    def now(self):
        return (self, self.n)


class Lane:

    def __init__(self):
        self.ops, self.seen = [], {}

    def __call__(self, method, *args, w=(), s=None, **kw):
        need = {}
        stack = [w]
        while stack:
            one = stack.pop()
            if one is None:
                continue
            if isinstance(one, tuple) and len(one) == 2 and isinstance(one[0], Sig):
                if self.seen.get(one[0], 0) < one[1]:
                    self.seen[one[0]] = need[one[0]] = one[1]
            else:
                stack.extend(one)
        self.ops.append((list(need.items()), method, args, kw, s))
        if s is None:
            return None
        s.n += s.step
        return s.now()

    def run(self, eng):
        for need, method, args, kw, s in self.ops:
            for sig, v in need:
                eng.wait_ge(sig.sem, v)
            ins = method(*args, **kw)
            if s is not None:
                ins.then_inc(s.sem, s.step)


class Bank:

    def __init__(self, ap):
        self.ap, self.free, self.busy = ap, [], False

    def freed(self, *tokens):
        self.free, self.busy = list(tokens), False


class Ring:

    def __init__(self, banks, flush):
        self.banks, self.n, self.flush = banks, 0, flush

    def next(self):
        self.n += 1
        b = self.banks[(self.n - 1) % len(self.banks)]
        while b.busy:
            self.flush()
        return b


def program(nc, x, meta, wall, wf, poolw, params, fng, bada, rel, out):
    units = plan()
    crows = nc.dram_tensor("c_rows", (8, TOK), F32, kind="Internal").ap()
    kept = nc.dram_tensor("x_kept", (4, 128, D), F32, kind="Internal").ap()
    A, V, G, T, SY = nc.scalar, nc.vector, nc.gpsimd, nc.tensor, nc.sync

    with ExitStack() as ctx:
        def sb(name, shape, dt=F32, where=ctx):
            return where.enter_context(nc.sbuf_tensor(name, shape, dt))

        sigs = {}

        def S(name, step=1):
            if name not in sigs:
                sigs[name] = Sig(ctx.enter_context(nc.semaphore("s_" + name)), step)
            return sigs[name]

        def DS(name):
            return S(name, 16)

        pe, act, dve, pool, sp = Lane(), Lane(), Lane(), Lane(), Lane()

        psum = ctx.enter_context(nc.psum_tensor("psum", [128, 8, 512], F32))
        banks = [Bank(psum[:, i, :]) for i in range(8)]

        NR, NH = 3, 2
        raw = sb("raw", [128, NR, UNIT])
        wh = sb("wh", [128, NH, UNIT], F32R)
        wl = sb("wl", [128, NH, UNIT], F32R)
        hh = sb("hh", [128, 8, TOK], F32R)
        hl = sb("hl", [128, 8, TOK], F32R)
        ah = sb("ah", [128, 8, SEQ], F32R)
        al = sb("al", [128, 8, SEQ], F32R)
        ident = sb("ident", [128, 128])
        ones = sb("ones", [128, TOK])
        blk = sb("blk", [128, 128])
        eps = sb("eps", [128, 1])
        mis = sb("mis", [128, 2112])
        gt = sb("gt", [128, 2, D])
        sgt = sb("sgt", [128, 2056])
        two = sb("two", [128, 2, SEQ])
        tmp = sb("tmp", [128, 2, SEQ])
        cols = sb("cols", [128, 4, 8])
        prm = sb("prm", [128, 39])
        cact = sb("cact", [128, 8])
        half = sb("half", [128, 16])
        sm = sb("sm", [128, 512])
        ccol = sb("ccol", [128, 4, 8])
        acc = mis[:, 0:2048]
        c_ng, c_ps, c_g1, c_g2, c_c, c_gqk, c_bf = (prm[:, 0:8], prm[:, 8:12], prm[:, 12:20], prm[:, 20:28],
                                                    prm[:, 28:36], prm[:, 36:38], prm[:, 38:39])

        pool(G.memset, ones[:, :], 1.0, s=S("p_const"))
        pool(G.memset, half[:, :], -0.5, s=S("p_const"))
        pool(G.memset, eps[:, :], EPS, s=S("p_const"))
        t = pool(G.memset, ident[:, :], 0.0, s=S("p_const"))
        pool(G.affine_select, out=ident[:, :], in_=ident[:, :], compare_op=ALU.not_equal, fill=1.0, base=0,
             pattern=[[-1, 128]], channel_multiplier=1, w=t, s=S("p_const"))
        t = pool(G.memset, blk[:, :], 0.0, s=S("p_const"))
        pool(G.memset, blk[0:64, 0:64], 1.0, w=t, s=S("p_const"))
        t_const = pool(G.memset, blk[64:128, 64:128], 1.0, w=t, s=S("p_const"))

        st = {"dma": 0, "split": 0, "w": 0, "use": 0, "rate": 0, "due": 0, "ring": None,
              "last": sum(u[0] != "ada" for u in units) - 1}
        bg = []
        landed, slot_free, parts_of, done, ada = {}, {}, {}, {}, {"free": None}

        def load():
            n = st["dma"]
            if n < len(units):
                st["dma"] += 1
                landed[n] = sp(SY.dma_start, raw[:, n % NR, :], wall[n], w=slot_free.get(n - NR),
                               s=DS(f"d_w{n % NR}"))

        def ada_unit(n):
            _, _, kt, g = units[n]

            def clear():
                ada_finish()
                t0 = pool(G.memset, acc, 0.0, w=ada["free"], s=S("p_acc"))
                ada["t"] = [sp(SY.dma_start, acc[0:1, :], bada[g:g + 1, :], w=t0, s=DS("d_bada"))] * 4

            def piece(i):
                def run():
                    c = slice(512 * i, 512 * i + 512)
                    ada["t"][i] = dve(V.scalar_tensor_tensor, acc[:, c], raw[:, n % NR, c], cact[:, kt:kt + 1],
                                      acc[:, c], ALU.mult, ALU.add, w=[landed[n], ada["t"][i], t_cact],
                                      s=S("v_acc"))
                    if i == 3:
                        slot_free[n] = ada["t"][3]
                        load()
                        if kt == 7:
                            ada["ready"] = (g, ada["t"][3])
                return run

            if kt == 0:
                bg.append(clear)
            bg.extend(piece(i) for i in range(4))

        def split_next():
            while st["split"] < len(units) and units[st["split"]][0] == "ada":
                st["split"] += 1
                ada_unit(st["split"] - 1)
            n = st["split"]
            if n >= len(units):
                return
            st["split"] += 1
            w = st["w"]
            st["w"] += 1
            i, parts = w % NH, parts_of.setdefault(w, [])

            def piece(j):
                c = slice(512 * j, 512 * j + 512)
                r = raw[:, n % NR, c]

                def upper():
                    parts.append([act(A.activation, wh[:, i, c], r, ACT.Copy, w=[landed[n], done.get(w - NH)],
                                      s=S("a_wh"))])

                def lower():
                    t = parts[j]
                    t.append(dve(V.tensor_tensor, wl[:, i, c], r, wh[:, i, c].bitcast(F32), ALU.subtract,
                                 w=[t[0], done.get(w - NH)], s=S("v_wl")))
                    if j == 3:
                        slot_free[n] = list(t)
                        load()
                return upper, lower

            (u0, l0), (u1, l1), (u2, l2), (u3, l3) = (piece(j) for j in range(4))
            bg.extend((u0, u1, l0, u2, l1, u3, l2, l3))

        mod_tok = {}

        def ada_finish():
            if "ready" not in ada:
                return
            ring = st["ring"]
            g, tk = ada.pop("ready")
            ends = []
            for hf in range(2):
                which = 2 * g + hf
                if which in (2, 5):
                    row = gt[:, which // 3, :]
                    for c in range(2):
                        b = ring.next()
                        t = pe(T.matmul, b.ap, ones[:, 0:128], acc[:, 1024 * hf + 512 * c:1024 * hf + 512 * c + 512],
                               start=True, stop=True, w=[tk, b.free, t_const], s=S("t_ada"))
                        t2 = act(A.activation, row[:, 512 * c:512 * c + 512], b.ap, ACT.Copy,
                                 w=[t, st["za"]], s=S("a_ada"))
                        b.free = [t2]
                else:
                    b = ring.next()
                    for c in range(8):
                        o = 1024 * hf + 128 * c
                        t = pe(T.matmul, b.ap[:, 2 * c:2 * c + 2], acc[:, o:o + 128], ones[:, 0:2], start=(c == 0),
                               stop=(c == 7), skip_group_check=True, w=[tk, b.free, t_const], s=S("t_ada"))
                    j = {0: 0, 1: 1, 3: 2, 4: 3}[which]
                    src = b.ap[:, 0:16].rearrange("p (a b) -> p a b", b=2)[:, :, 0]
                    if which in (0, 3):
                        t2 = dve(V.tensor_copy, cols[:, j, :], src, w=t, s=S("v_ada"))
                    else:
                        t2 = dve(V.scalar_tensor_tensor, cols[:, j, :], src, 1.0, c_g1 if which == 1 else c_g2,
                                 ALU.add, ALU.mult, w=[t, t_small], s=S("v_ada"))
                    b.free = [t2]
                ends.append(t)
                mod_tok[which] = t2
            ada["free"] = ends

        queue, pend = [], []

        def flush():
            for g in list(pend):
                if next(g, True):
                    pend.remove(g)

        def rotating(bk):
            return Ring(bk, flush)

        def begin(g):
            next(g)
            pend.append(g)

        def settle():
            while pend:
                flush()

        def pump(left):
            for _ in range(-(-len(bg) // max(left, 1))):
                bg.pop(0)()

        def fill(n):
            st["due"] += n
            while st["due"] >= 1:
                st["due"] -= 1
                if queue:
                    queue.pop(0)()

        def drain():
            while queue:
                queue.pop(0)()
            settle()

        class Parts:

            def __init__(self, w):
                self.parts = parts_of[w]

            def __getitem__(self, j):
                while len(self.parts) <= j or len(self.parts[j]) < 2:
                    bg.pop(0)()
                return self.parts[j]

        class Unit:

            def __init__(self):
                w = self.w = st["use"]
                st["use"] += 1
                self.h, self.l = wh[:, w % NH, :], wl[:, w % NH, :]
                while st["w"] <= min(w + 1, st["last"]):
                    split_next()
                self.t, self.left = Parts(w), 8

            def slot(self):
                if self.left:
                    pump(self.left)
                    self.left -= 1
                if self.left == 4:
                    ada_finish()

            def over(self, t):
                done[self.w] = t
                pump(1)

        def three(bank, lh, ll, rh, rl, first, last, w=None, s=None):
            pe(T.matmul, bank, lh, rh, start=first, stop=False, skip_group_check=True, w=w)
            pe(T.matmul, bank, lh, rl, start=False, stop=False, skip_group_check=True)
            return pe(T.matmul, bank, ll, rh, start=False, stop=last, skip_group_check=True, s=s)

        def group_cols(u, bank, src, src_tok, sub=0, base=None, nk=8, c0=0, n=SEQ, k0=0):
            for k in range(nk):
                o = (k * 256 + sub * 128) if base is None else base + 128 * k
                t = three(bank.ap[:, 0:n], u.h[:, o:o + 128], u.l[:, o:o + 128], src[0][:, k0 + k, c0:c0 + n],
                          src[1][:, k0 + k, c0:c0 + n], k == 0, k == nk - 1,
                          w=[src_tok[k0 + k], u.t[o // 512], bank.free if k == 0 else None],
                          s=S("t_mm") if k == nk - 1 else None)
                if n == SEQ:
                    if k % 2:
                        u.slot()
                    fill(st["rate"])
            return t

        def group_rows(src, src_tok, tiles, bank_of, evac, khs=(0, 1), before=None, mid=None):
            for kh in khs:
                if mid and kh == khs[1]:
                    mid()
                u = Unit()
                outer = before is not None and kh == khs[0]
                n = len(tiles)
                for i, k in ([(i, k) for k in range(4) for i in range(n)] if outer
                             else [(i, k) for i in range(n) for k in range(4)]):
                    c0, b = tiles[i], bank_of[i]
                    kk = 4 * kh + k
                    if before and i == 0:
                        before(kk)
                    t = three(b.ap, src[0][:, kk, c0:c0 + 128], src[1][:, kk, c0:c0 + 128],
                              u.h[:, 512 * k:512 * k + 512], u.l[:, 512 * k:512 * k + 512],
                              kh == khs[0] and k == 0, kh == khs[1] and k == 3,
                              w=[src_tok[kk], u.t[k], b.free if kh == khs[0] and k == 0 else None],
                              s=S("t_mm") if k == 3 else None)
                    if k % 2:
                        u.slot()
                    if k == 3 and kh == khs[1]:
                        evac(i, b, t)
                    fill(st["rate"])
                u.over(t)
            return t

        def split_sb(hi, lo, src, w):
            t1 = act(A.activation, hi, src, ACT.Copy, w=w, s=S("a_hi"))
            return [t1, dve(V.tensor_tensor, lo, src, hi.bitcast(F32), ALU.subtract, w=[t1, w], s=S("v_lo"))]

        def rstd(w, i, n, inv, rows=128):
            v = sm[0:rows, i:i + n]
            t = pool(G.tensor_scalar, v, v, inv, EPS, ALU.mult, ALU.add, w=w, s=S("p_ms"))
            return pool(G.tensor_tensor, v, v, half[0:rows, 0:n], ALU.pow, w=[t, t_const], s=S("p_rstd"))

        def square_sum(src, i, w, rows=128):
            j = tmp[0:rows, :, :].rearrange("p a b -> p (a b)")
            return act(A.activation, j, src, ACT.Square, accum_out=sm[0:rows, i:i + 1],
                       w=[w, S("a_sq").now(), S("v_tmp").now()], s=S("a_sq"))

        def transposed(tiles, ring, take):
            toks = {}

            def one(kt):
                b = ring.next()
                for i, (src, tk) in enumerate(tiles):
                    t = pe(T.transpose, b.ap[:, 128 * i:128 * i + 128], src[:, 128 * kt:128 * kt + 128],
                           ident[:, :], w=[tk, t_const, b.free if i == 0 else None],
                           s=S("t_tp") if i == len(tiles) - 1 else None)
                toks[kt] = take(kt, b, t)

            def ahead(kt):
                while len(toks) < min(8, kt + 4):
                    one(len(toks))
            return toks, ahead

        first = ExitStack()
        xt = sb("xt", [128, 4, D], where=first)
        xm = sb("xm", [META, D], where=first)
        wfb = sb("wfb", [128, 8, 128], where=first)
        wfh = sb("wfh", [128, 8, 128], F32R, where=first)
        wfl = sb("wfl", [128, 8, 128], F32R, where=first)
        fa, fe, fc = (sgt[:, TOK * i:TOK * i + TOK] for i in range(3))
        t_m = act(A.dma_start, xm[:, :], meta, s=DS("d_xm"))
        t_small = act(A.dma_start, prm[:, :], params, s=DS("d_small"))
        t_x = [sp(SY.dma_start, xt[:, i, :], x[128 * i:128 * i + 128, :], s=DS(f"d_x{i}")) for i in range(4)]
        t_wf = act(A.dma_start, wfb[:, :, :], wf, s=DS("d_wf"))
        for _ in range(NR):
            load()

        normed = []
        for i, (src, tk, rows) in enumerate([(xm[:, :], t_m, META)] + [(xt[:, i, :], t_x[i], 128) for i in range(4)]):
            t = square_sum(src, 310 + i, tk, rows)
            r = rstd(t, 310 + i, 1, 1.0 / D, rows)
            t2 = dve(V.tensor_scalar, src, src, sm[0:rows, 310 + i:311 + i], None, ALU.mult, w=r, s=S("v_xn"))
            normed.append((src, t2))
        bm = banks[4]
        for kt in range(8):
            t = pe(T.transpose, bm.ap[:, 16 * kt:16 * kt + 16], xm[:, 128 * kt:128 * kt + 128],
                   ident[0:META, 0:META], w=[normed[0][1], t_const], s=S("t_tp"))
        for kt in range(8):
            t1 = act(A.activation, hh[:, kt, 0:META], bm.ap[:, 16 * kt:16 * kt + 16], ACT.Copy,
                     scale=c_ng[:, kt:kt + 1], w=[t, t_small], s=S("a_hi"))
        for kt in range(8):
            t_hm = dve(V.scalar_tensor_tensor, hl[:, kt, 0:META], bm.ap[:, 16 * kt:16 * kt + 16],
                       c_ng[:, kt:kt + 1], hh[:, kt, 0:META].bitcast(F32), ALU.mult, ALU.subtract, w=[t1, t],
                       s=S("v_lo"))
        bm.free = [t1, t_hm]

        def take_first(kt, b, t):
            g, o = c_ng[:, kt:kt + 1], hh[:, kt, META:TOK]
            t1 = act(A.activation, o, b.ap, ACT.Copy, scale=g, w=t, s=S("a_hi"))
            t2 = dve(V.scalar_tensor_tensor, hl[:, kt, META:TOK], b.ap, g, o.bitcast(F32), ALU.mult,
                     ALU.subtract, w=[t1, t], s=S("v_lo"))
            b.free = [t1, t2]
            return [t1, t2, t_hm]

        h_tok, ahead = transposed(normed[1:], rotating([banks[5], banks[6], banks[4]]), take_first)
        hs = (hh, hl)
        tw = split_sb(wfh[:, :, :], wfl[:, :, :], wfb[:, :, :], t_wf)

        at_tok, at_free = {}, [None]

        class Att:

            def __init__(self, kind, m, v2, p_sb, pt, tring, oring, sring, ybase, after=None):
                self.kind, self.m, self.v2, self.p, self.pt = kind, m, v2, p_sb, pt
                self.tring, self.oring, self.sring, self.ybase = tring, oring, sring, ybase
                self.off = [sum(m + 128 * (j + 1) for j in range(i)) for i in range(4)]
                self.ptoff = {0: 0, 1: 512, 2: 896, 3: 1152, -1: 1280}
                self.qk, self.extra, self.za = {}, {}, {}
                self.tok, self.used = {}, {}
                self.h0 = after.h0 + 8 if after else 0
                self.pused, self.ptt, self.ptused, self.o = ((after.pused, after.ptt, after.ptused, after.o) if after
                                                             else ({}, {}, {}, {}))
                self.vfree, self.vtok, self.pfree = None, None, None
                self.pair_over = {}
                self.prepare, self.begun = None, set()

            def score(self, h, i):
                m, kind, n = self.m, self.kind, 128 * (i + 1)
                if i == 3 and h < 7 and self.prepare:
                    self.prepare(h + 1)
                par = 64 * (h % 2)
                self.begun.add(4 * h + i)
                while len(self.qk[h // 2][2]) < 2:
                    flush()
                q, k, ready = self.qk[h // 2]
                ql = q[par:par + 64, 128 * i:128 * i + 128]
                P = self.p[:, h % 2, self.off[i]:self.off[i] + m + n]
                b = self.sring.next()
                over = [b]
                kp = k[par:par + 64, 0:m + n]
                if m + n <= 512:
                    sc = b.ap[:, 0:m + n]
                    t = pe(T.matmul, sc, ql, kp, start=True, stop=True, skip_group_check=True,
                           w=[ready, b.free], s=S("t_sc"))
                else:
                    while banks[4].busy or banks[5].busy:
                        flush()
                    over, c = [banks[4], banks[5]], (m + n) // 2
                    sc = psum[:, 4:6, :].rearrange("p a b -> p (a b)")[:, 512 - c:512 + c]
                    pe(T.matmul, sc[:, 0:c], ql, kp[:, 0:c], start=True, stop=True, skip_group_check=True,
                       w=[ready, [o.free for o in over]])
                    t = pe(T.matmul, sc[:, c:2 * c], ql, kp[:, c:2 * c], start=True, stop=True,
                           skip_group_check=True, s=S("t_sc"))
                self.pair_over[h // 2] = t
                for o in over:
                    o.busy = True
                old_p = [self.pused.get(self.h0 + h - 2), self.pfree]
                c = 320 + 4 * ((4 * h + i) % 16)
                mx, su, nmx = sm[:, c:c + 1], sm[:, c + 1:c + 2], sm[:, c + 2:c + 3]
                old = self.tok.get(4 * h + i - 16)
                diag = P[:, m + n - 128:m + n]
                if kind == "sb":
                    g = self.extra[(4 * h + i) % 2]
                    while g["busy"]:
                        flush()
                    g["busy"] = True
                    yield
                    gg = g["ap"][:, 512 - n:512]
                    t1 = act(A.activation, P, sc, ACT.Sigmoid, w=[t, old_p], s=S("a_s"))
                    t1b = act(A.activation, gg, sc, ACT.Sigmoid, scale=-1.0, w=g["free"], s=S("a_s"))
                    b.freed(t1b)
                    t2a = pool(G.affine_select, out=diag, in_=diag, compare_op=ALU.is_gt, fill=0.0, base=0,
                               pattern=[[-1, 128]], channel_multiplier=1, w=t1, s=S("p_s"))
                    gd = g["ap"][:, 384:512]
                    t2 = pool(G.affine_select, out=gd, in_=gd, compare_op=ALU.is_gt, fill=1.0, base=0,
                              pattern=[[-1, 128]], channel_multiplier=1, w=t1b, s=S("p_s"))
                    yield
                    yield
                    t3 = dve(V.tensor_tensor_scan, gg[:, ::-1], gg[:, ::-1], ones[:, 0:n], 1.0, ALU.mult, ALU.mult,
                             w=[t2, t1b, t_const], s=S("v_s"))
                    yield
                    t4 = dve(V.tensor_tensor, P, P, g["ap"][:, 513 - n:513], ALU.mult, w=[t3, t2, g["one"]],
                             s=S("v_p"))
                    g["free"], g["busy"] = [t4], False
                    self.tok[4 * h + i] = t4
                    return
                yield
                t2 = None
                if kind == "fg":
                    cb, cbt = self.extra[h]
                    t1 = dve(V.scalar_tensor_tensor, P, sc, ccol[:, i, h:h + 1], cb[:, 0:m + n], ALU.add,
                             ALU.subtract, w=[t, old_p, cbt, t_cc], s=S("v_s"))
                    t2 = pool(G.affine_select, out=diag, in_=diag, compare_op=ALU.is_ge, fill=NEG, base=0,
                              pattern=[[-1, 128]], channel_multiplier=1, w=t1, s=S("p_s"))
                else:
                    bt, btt = self.extra[h]
                    t1 = dve(V.tensor_tensor_reduce, out=P, in0=sc, in1=bt[:, 512 - n:512], scale=1.0,
                             scalar=-3.0e38, op0=ALU.add, op1=ALU.max, accum_out=mx, w=[t, old_p, btt, old],
                             s=S("v_s"))
                for o in over:
                    o.freed(t1)
                self.used[h] = t1
                yield
                if kind == "fg":
                    t3 = dve(V.tensor_reduce, nmx, P, AX.X, ALU.max, negate=True, w=[t2, old], s=S("v_m"))
                else:
                    t3 = dve(V.tensor_scalar, nmx, mx, -1.0, None, ALU.mult, w=t1, s=S("v_m"))
                yield
                t4 = act(A.activation, P, P, ACT.Exp, bias=nmx, accum_out=su, w=[t3, t1, t2], s=S("a_s"))
                yield
                t5 = dve(V.reciprocal, mx, su, w=t4, s=S("v_m"))
                yield
                self.tok[4 * h + i] = act(A.activation, P, P, ACT.Copy, scale=mx, w=[t5, t4], s=S("a_p"))

            def turn(self, h, j):
                b = self.tring.next()
                i0, rows, w = max(j, 0), (128 if j >= 0 else META), 512 - 128 * max(j, 0)
                for i in range(i0, 4):
                    o = self.off[i] + (self.m + 128 * j if j >= 0 else 0)
                    t = pe(T.transpose, b.ap[:, 128 * (i - i0):128 * (i - i0) + 128], self.p[:, h % 2, o:o + 128],
                           ident[:, :], w=[self.tok[4 * h + i], b.free if i == i0 else None],
                           s=S("t_tp") if i == 3 else None)
                self.pused[self.h0 + h] = t
                b.busy = True
                o = self.ptoff[j]
                ph, pl = self.pt
                old = [self.ptused.get(j), self.pfree]
                yield
                t1 = act(A.activation, ph[0:rows, o:o + w], b.ap[0:rows, 0:w], ACT.Copy, w=[t, old], s=S("a_pt"))
                yield
                t2 = dve(V.tensor_tensor, pl[0:rows, o:o + w], b.ap[0:rows, 0:w], ph[0:rows, o:o + w].bitcast(F32),
                         ALU.subtract, w=[t1, t, old], s=S("v_pt"))
                b.freed(t1, t2)
                self.ptt[j] = [t1, t2]

            def value(self, h, j):
                i0, rows, w, o = max(j, 0), (128 if j >= 0 else META), 512 - 128 * max(j, 0), self.ptoff[j]
                ph, pl = self.pt
                lhs = self.v2[0:rows, (j if j >= 0 else 4), h, :]
                end = j == (-1 if self.m else 0)
                if j == 3:
                    self.o["bank"] = self.oring.next()
                b = self.o["bank"]
                pe(T.matmul, b.ap[:, 128 * i0:512], lhs, ph[0:rows, o:o + w], start=(j == 3), stop=False,
                   skip_group_check=True, w=[self.ptt.pop(j), self.vtok, b.free if j == 3 else None])
                t = pe(T.matmul, b.ap[:, 128 * i0:512], lhs, pl[0:rows, o:o + w], start=False, stop=end,
                       skip_group_check=True, s=S("t_pv"))
                self.ptused[j] = t
                if end:
                    b.busy = True
                    begin(self.output(h, b, t))

            def output(self, h, b, t):
                par, o, p = 64 * (h % 2), tmp[:, 1, :], self.ybase + h // 2
                yield
                t1 = act(A.activation, tmp[0:64, 0, :], b.ap[64:128, :], ACT.Copy,
                         w=[t, S("v_tmp").now(), S("a_sq").now()], s=S("a_o"))
                yield
                t2 = dve(V.tensor_tensor, tmp[par:par + 64, 1, :], b.ap[0:64, :], tmp[0:64, 0, :], ALU.add,
                         w=[t1, t, self.o.get(0)], s=S("v_tmp"))
                b.freed(t1, t2)
                if not par:
                    return
                yield
                if self.kind == "fg":
                    z, zt = self.za[h // 2]
                    t2 = dve(V.tensor_tensor, o, o, z, ALU.mult, w=[t2, zt], s=S("v_tmp"))
                    yield
                t1 = act(A.activation, ah[:, p, :], o, ACT.Copy, w=[t2, at_free[0]], s=S("a_hi"))
                yield
                t2 = dve(V.tensor_tensor, al[:, p, :], o, ah[:, p, :].bitcast(F32), ALU.subtract,
                         w=[t1, t2, at_free[0]], s=S("v_lo"))
                self.o[0] = at_tok[p] = [t1, t2]

        lag, last_head = [], []

        def do_score(att, h, i):
            def run():
                flush()
                begin(att.score(h, i))
            return run

        def do_turn(att, h, j):
            def run():
                flush()
                while any(4 * h + i not in att.tok for i in range(max(j, 0), 4)):
                    flush()
                begin(att.turn(h, j))
            return run

        def do_value():
            def run():
                flush()
                att, h, j = lag.pop(0)
                while j not in att.ptt:
                    flush()
                att.value(h, j)
            return run

        def push_head(att, h):
            scores = [do_score(att, h, i) for i in (3, 2, 1, 0)] if att else []
            if last_head:
                a, ph = last_head.pop()
                for j in [3, 2, 1, 0] + ([-1] if a.m else []):
                    queue.append(do_turn(a, ph, j))
                    queue.append(lambda x=(a, ph, j): lag.append(x) or (len(lag) > 2 and do_value()()))
                    if scores:
                        queue.append(scores.pop(0))
            queue.extend(scores)
            if att:
                last_head.append((att, h))
            else:
                queue.extend([lambda: lag and do_value()()] * 2)

        def push_pair(att, p):
            push_head(att, 2 * p)
            push_head(att, 2 * p + 1)

        def scored(att, p):
            while p >= 0 and any(4 * h + i not in att.begun for h in (2 * p, 2 * p + 1) for i in range(4)):
                queue.pop(0)()

        def value_parts(att, rows_of):
            def evac(i, b, t):
                r = rows_of[i]
                src = b.ap[0:r, :].rearrange("p (h c) -> p h c", h=8)
                hi, lo = att.v2[0:r, i, :, 0:64], att.v2[0:r, i, :, 64:128]
                t1 = act(A.activation, hi, src, ACT.Copy, w=[t, att.vfree()], s=S("a_hi"))
                t2 = dve(V.tensor_tensor, lo, src, hi.bitcast(F32), ALU.subtract, w=[t1, t, att.vfree()],
                         s=S("v_lo"))
                b.free = [t1, t2]
                att.vtok = [t1, t2]
            return evac

        ub, us, pw = mis[:, 0:528], (mis[:, 528:1056], mis[:, 1056:1584]), mis[:, 1584:2096]
        za = gt.rearrange("p a b -> p (a b)").rearrange("p (a b) -> p a b", a=4)
        zp = two
        t_pw = act(A.dma_start, pw, poolw, s=DS("d_pw"))
        first.close()

        b1 = ExitStack()
        v2 = sb("v2", [128, 5, 8, 128], F32R, where=b1)
        p_sb = sb("p_sb", [128, 2, 4 * META + 1280], where=b1)
        pth = sb("pth", [128, 1280 + SEQ], F32R, where=b1)
        ptl = sb("ptl", [128, 1280 + SEQ], F32R, where=b1)
        q_sb = sb("q_sb", [128, 2, SEQ], where=b1)
        k_sb = sb("k_sb", [128, 2, TOK], where=b1)
        cb = sb("cb", [128, 2, TOK], where=b1)

        tring = rotating([banks[3], banks[6]])
        fg = Att("fg", META, v2, p_sb, (pth, ptl), tring, rotating([banks[2], banks[7]]), rotating([banks[4], banks[5]]), 4)
        fg.vfree = lambda: S("t_tp").now()

        def row_of_c(h):
            i = h % 2
            fg.extra[h] = (cb[:, i, :], sp(SY.dma_start, cb[:, i, :], crows[h:h + 1, :].to_broadcast([128, TOK]),
                                           w=[t_crow, first_over, fg.used.get(h - 2)], s=DS(f"d_cb{i}")))
        fg.prepare = row_of_c

        group_rows(hs, h_tok, [META, META + 128, META + 256, META + 384, 0], banks[0:4] + [banks[7]],
                   value_parts(fg, [128, 128, 128, 128, META]), before=ahead)
        pr = rotating(banks[0:2])

        t = act(A.activation, sm[:, 300:308], c_c, ACT.Sigmoid, w=t_small, s=S("a_c"))
        t_cact = dve(V.tensor_tensor, cact[:, :], c_c, sm[:, 300:308], ALU.mult, w=[t, t_small], s=S("v_c"))

        fb, fmb = banks[5], banks[6]
        for (b, c0, n) in ((fmb, 0, META), (fb, META, SEQ)):
            for k in range(8):
                t = three(b.ap[:, 0:n], wfh[:, k, :], wfl[:, k, :], hh[:, k, c0:c0 + n], hl[:, k, c0:c0 + n],
                          k == 0, k == 7, w=[tw, h_tok[k], b.free], s=S("t_mm") if k == 7 else None)
        dve(V.tensor_scalar, fa[:, 0:META], fmb.ap[:, 0:META], c_bf, None, ALU.add, w=[t, t_small], s=S("v_f"))
        ta = dve(V.tensor_scalar, fa[:, META:TOK], fb.ap, c_bf, None, ALU.add, w=t, s=S("v_f"))
        fb.free, fmb.free = [ta], [ta]
        tb = act(A.activation, fe[:, :], fa[:, :], ACT.Abs, w=ta, s=S("a_f"))
        tb = act(A.activation, fe[:, :], fe[:, :], ACT.Exp, scale=-1.0, w=tb, s=S("a_f"))
        tb = act(A.activation, fe[:, :], fe[:, :], ACT.Ln, bias=1.0, w=tb, s=S("a_f"))
        ta = dve(V.scalar_tensor_tensor, fa[:, :], fa[:, :], 0.0, fe[:, :], ALU.min, ALU.subtract, w=[ta, tb],
                 s=S("v_f"))
        ta = dve(V.tensor_tensor_scan, fc[:, :], ones[:, :], fa[:, :], 0.0, ALU.mult, ALU.add, w=[ta, t_const],
                 s=S("v_f"))
        t_crow = sp(SY.dma_start, crows, fc[0:8, :], w=ta, s=DS("d_c"))
        first_over = [S("t_tp").now(), S("t_mm").now()]
        fg.pfree = first_over
        row_of_c(0)

        def columns_of_c():
            for i in range(4):
                t = pe(T.transpose, fb.ap[:, 128 * i:128 * i + 128], fc[:, META + 128 * i:META + 128 * i + 128],
                       ident[:, :], w=[ta, fb.free], s=S("t_tp"))
            t2 = dve(V.tensor_copy, ccol[:, :, :], fb.ap.rearrange("p (i c) -> p i c", i=4)[:, :, 0:8], w=t,
                     s=S("v_cc"))
            fb.free = [t2]
            return t, t2

        def gate(dst, b, t, w):
            t1 = act(A.activation, dst, b.ap, ACT.Sigmoid, w=[t, w], s=S("a_z"))
            t2 = dve(V.tensor_tensor, dst, b.ap, dst, ALU.mult, w=[t1, t], s=S("v_z"))
            b.free = [t1, t2]
            return t2

        for j in range(2):
            u = Unit()
            for sub in range(2):
                b = pr.next()
                t = group_cols(u, b, hs, h_tok, sub, c0=META)
                fg.za[2 * j + sub] = (za[:, 2 * j + sub, :], gate(za[:, 2 * j + sub, :], b, t, None))
            u.over(t)
            if j == 0:
                t_cp, t_cc = columns_of_c()

        def group_all(u, sub, dst, w):
            both, n = [pr.next(), tring.next()], TOK // 2
            fg.tring = rotating([b for b in tring.banks if b is not both[1]])
            for k in range(8):
                o = k * 256 + sub * 128
                for i, b in enumerate(both):
                    t = three(b.ap[:, 0:n], u.h[:, o:o + 128], u.l[:, o:o + 128], hh[:, k, n * i:n * i + n],
                              hl[:, k, n * i:n * i + n], k == 0, k == 7,
                              w=[h_tok[k], u.t[o // 512], b.free if k == 0 else None],
                              s=S("t_mm") if k == 7 else None)
                if k % 2:
                    u.slot()
                fill(st["rate"])
            for i, b in enumerate(both):
                b.free = [act(A.activation, dst[:, n * i:n * i + n], b.ap[:, 0:n], ACT.Copy, w=[t, w], s=S("a_m"))]
            fg.tring = tring
            return both[1].free[0], t

        st["rate"] = 1
        late = []

        def project_qk(p):
            i = p % 2
            u = Unit()
            scored(fg, p - 2)
            old = [fg.pair_over.get(p - 2), first_over]
            b = pr.next()
            t = group_cols(u, b, hs, h_tok, 0, c0=META)
            tq = act(A.activation, q_sb[:, i, :], b.ap, ACT.Copy, scale=0.125, w=[t, old], s=S("a_q"))
            b.free = [tq]
            tk, t = group_all(u, 1, k_sb[:, i, :], old)
            u.over(t)
            fg.qk[p] = (q_sb[:, i, :], k_sb[:, i, :], [tq, tk])
            push_pair(fg, p)

        def project_uz(p):
            i = p % 2
            u = Unit()
            if late:
                queue.insert(min(3, len(queue)), late.pop())
            tu, t = group_all(u, 0, ub, used["ub"])
            src, lo, tt = ub, 0, [tu, used["us"]]
            for s_ in range(p + 1):
                dst, dd = us[s_ % 2], 1 << s_
                lo += dd
                tt = dve(V.tensor_tensor, dst[:, lo:TOK], src[:, lo:TOK], src[:, lo - dd:TOK - dd], ALU.add,
                         w=tt, s=S("v_u"))
                src = dst
            pd = us[(p + 1) % 2][:, META:TOK]
            tt = dve(V.scalar_tensor_tensor, pd, src[:, META:TOK], 1.0 / (2 << p), ub[:, META:TOK], ALU.mult,
                     ALU.subtract, w=tt, s=S("v_u"))
            used["ub"] = tt
            b = pr.next()
            t = group_cols(u, b, hs, h_tok, 1, c0=META)
            u.over(t)
            yo = zp[:, i, :]
            tz = gate(yo, b, t, used.get(("zp", p - 2)))

            def product():
                b = tring.next()
                t = pe(T.matmul, b.ap, pw[:, 128 * p:128 * p + 128], pd, start=True, stop=True,
                       w=[tt, t_pw, b.free], s=S("t_y"))
                used["us"] = t
                t3 = dve(V.scalar_tensor_tensor, yo, b.ap, c_ps[:, p:p + 1], yo, ALU.mult, ALU.mult, w=[t, tz],
                         s=S("v_y"))
                b.free = [t3]
                used["zp", p] = at_tok[p] = split_sb(ah[:, p, :], al[:, p, :], yo, t3)
            late.append(product)

        used = {"us": None, "ub": None}
        for kind, p in ORDER_1:
            if kind == "qk":
                project_qk(p)
            else:
                project_uz(p)
        push_head(None, None)
        late.pop()()
        ada["free"] = [used["us"], used["ub"]]

        sg = sgt[:, 0:2048].rearrange("p (a b) -> p a b", a=4)
        mt = two
        sg_used = {n: [t_crow, t_cp] for n in range(4)}
        mt_used, m_tok = used["zp", 3], {}
        for e_ in range(4):
            sgo = {}
            for dd in range(2):
                u = Unit()
                for sub in range(2):
                    b = pr.next()
                    t = group_cols(u, b, hs, h_tok, sub, c0=META)
                    n = 2 * dd + sub
                    sgo[n] = act(A.activation, sg[:, n, :], b.ap, ACT.Sigmoid, w=[t, sg_used.get(n)], s=S("a_g"))
                    b.free = [sgo[n]]
                u.over(t)
            if e_ == 0:
                drain()
                st["rate"] = 0
                b1.close()
                b1_over = [S("t_pv").now(), S("t_tp").now(), S("a_pt").now(), S("v_pt").now(), at_tok[7],
                           S("v_s").now()]
                st["za"] = at_tok[7]
                w1 = ExitStack()
                x1 = sb("x1", [128, 4, D], where=w1)
                gf = sb("gf", [128, D], where=w1)
                w1a = ExitStack()
                mh = sb("mh", [128, 8, SEQ], F32R, where=w1a)
                ml = sb("ml", [128, 8, SEQ], F32R, where=w1a)
                t_x1 = [sp(SY.dma_start, x1[:, i, :], x[128 * i:128 * i + 128, :], w=b1_over, s=DS(f"d_x{i}"))
                        for i in range(4)]
                t_gf = sp(SY.dma_start, gf[:, :], fng.to_broadcast([128, D]), w=b1_over, s=DS("d_gf"))
                st["ring"] = rotating([banks[3], banks[6]])
            u = Unit()
            for dd in range(2):
                n = 2 * e_ + dd
                b = pr.next()
                t = group_cols(u, b, (ah, al), at_tok, base=dd * 1024, nk=4)
                t1 = dve(V.tensor_tensor, mt[:, 0, :], b.ap, sg[:, 2 * dd, :], ALU.mult,
                         w=[t, sgo[2 * dd], mt_used], s=S("v_m1"))
                b.free = [t1]
                b = pr.next()
                t = group_cols(u, b, (ah, al), at_tok, base=dd * 1024 + 512, nk=4, k0=4)
                t2 = dve(V.tensor_tensor, mt[:, 1, :], b.ap, sg[:, 2 * dd + 1, :], ALU.mult,
                         w=[t, sgo[2 * dd + 1], mt_used], s=S("v_m1"))
                b.free = [t2]
                sg_used[2 * dd], sg_used[2 * dd + 1] = t1, t2
                t3 = dve(V.tensor_tensor, mt[:, 0, :], mt[:, 0, :], mt[:, 1, :], ALU.add, w=[t1, t2], s=S("v_m1"))
                mt_used = m_tok[n] = split_sb(mh[:, n, :], ml[:, n, :], mt[:, 0, :], [t3, b1_over])
            u.over(t)
        at_free[0] = t

        t1s, normed, chains, t_kept, m_over = {}, {}, [], [], []

        def tick():
            for g in list(chains):
                if next(g, True):
                    chains.remove(g)

        def both_norms(i):
            xi = x1[:, i, :]
            t = square_sum(xi, 384 + i, [t1s[i, 0], t1s[i, 1]])
            yield
            r = rstd(t, 384 + i, 1, 1.0 / D)
            yield
            t = dve(V.scalar_tensor_tensor, xi, xi, sm[:, 384 + i:385 + i], gf[:, :], ALU.mult, ALU.mult,
                    w=[r, t_gf, t1s[i, 1]], s=S("v_xn"))
            t_kept.append(sp(SY.dma_start, kept[i], xi, w=t, s=DS(f"d_k{i}")))
            yield
            t2 = square_sum(xi, 388 + i, t)
            yield
            r = rstd(t2, 388 + i, 1, 1.0 / D)
            yield
            t = dve(V.tensor_scalar, xn[:, i, :], xi, sm[:, 388 + i:389 + i], None, ALU.mult, w=[r, m_over[0], t],
                    s=S("v_xn"))
            normed[i] = (xn[:, i, :], t)

        def evac_out(ch):
            def evac(i, b, t):
                o = x1[:, i, 512 * ch:512 * ch + 512]
                t1s[i, ch] = dve(V.tensor_tensor, o, b.ap, o, ALU.add, w=[t, t_x1[i]], s=S("v_r"))
                b.free = [t1s[i, ch]]
                if ch:
                    tick()
                    chains.append(both_norms(i))
            return evac

        for ch in range(2):
            bk = banks[0:4] if ch == 0 else [banks[4], banks[5], banks[7], banks[3]]
            st["ring"] = rotating([banks[6]])
            t = group_rows((mh, ml), m_tok, [0, 128, 256, 384], bk, evac_out(ch))
        w1a.close()
        xn = sb("xn", [128, 4, D], where=w1)
        m_over.append(t)
        while chains:
            tick()

        def take_mod(j, old):
            def take(kt, b, t):
                o, d = kt % 2, two[:, kt % 2, :]
                t0 = dve(V.tensor_scalar, d, b.ap, cols[:, j + 1, kt:kt + 1], cols[:, j, kt:kt + 1], ALU.mult,
                         ALU.add, w=[t, mod_tok[{0: 0, 2: 3}[j]], mod_tok[{0: 1, 2: 4}[j]], two_used[o]],
                         s=S("v_two"))
                b.free = [t0]
                two_used[o] = split_sb(hh[:, kt, 0:SEQ], hl[:, kt, 0:SEQ], d, [t0, old])
                return two_used[o]
            return take

        two_used = [mt_used, mt_used]
        h_tok, ahead = transposed([normed[i] for i in range(4)], rotating(banks[0:4]), take_mod(0, m_over))
        w1.close()
        st["ring"] = rotating([banks[3]])

        b2 = ExitStack()
        v_ca = sb("v_ca", [128, 4, 8, 128], F32R, where=b2)
        v_sb = sb("v_sb", [128, 4, 8, 128], F32R, where=b2)
        p_sb = sb("p_sb2", [128, 2, 1280], where=b2)
        pth = sb("pth2", [128, 1280], F32R, where=b2)
        ptl = sb("ptl2", [128, 1280], F32R, where=b2)
        q_sb = sb("q_sb2", [128, 2, SEQ], where=b2)
        k_sb = sb("k_sb2", [128, 2, SEQ], where=b2)
        bt = (sgt[:, 0:512], sgt[:, 512:1024])
        gb = (sgt[:, 1024:1537], sgt[:, 1538:2051])
        sq = two

        pr = rotating(banks[0:2])
        tring, oring, sring = rotating([banks[3], banks[6]]), rotating([banks[2], banks[7]]), rotating([banks[4], banks[5]])
        ca = Att("ca", 0, v_ca, p_sb, (pth, ptl), tring, oring, sring, 4)
        sbk = Att("sb", 0, v_sb, p_sb, (pth, ptl), tring, oring, sring, 0, after=ca)

        def norm_over():
            return [t_kept, S("t_tp").now(), S("a_sq").now(), S("v_xn").now()]
        ca.vfree = norm_over

        def table(h):
            i = h % 2
            t = sp(SY.dma_start, bt[i], rel[h], w=[sg_used[0], sg_used[1], ca.used.get(h - 2)], s=DS(f"d_bt{i}"))
            ca.extra[h] = (bt[i], pool(G.memset, bt[i][0:64, 448:512], NEG, w=t, s=S("p_bt")))
        ca.prepare = table
        table(0)

        hs2 = (hh, hl)
        group_rows(hs2, h_tok, [0, 128, 256, 384], [banks[4], banks[5], banks[7], banks[6]],
                   value_parts(ca, [128] * 4), before=ahead)
        x1_over = norm_over()
        sbk.vfree = lambda: x1_over
        ca.pfree = sbk.pfree = x1_over
        st["rate"] = RATE_CA
        qs = [(q_sb[:, i, :], k_sb[:, i, :]) for i in range(2)] + [(mis[:, 1024:1536], mis[:, 1536:2048])]

        def place(g):
            if g >= 3:
                att, p = (ca, g - 3) if g < 7 else (sbk, g - 7)
                scored(att, p)
                return qs[g % 3], att.pair_over[p]
            return qs[g % 3], [x1_over, ada["free"]]

        def other_banks():
            settle()
            mine = ca.o["bank"]
            bk = [banks[0], banks[1], banks[3], banks[2] if mine is banks[7] else banks[7]]
            return mine, bk
        one = [pool(G.memset, gb[i][:, 512:513], 1.0, w=[sg_used[2], sg_used[3]], s=S("p_bt")) for i in range(2)]
        sbk.extra = {i: {"ap": gb[i], "free": None, "busy": False, "one": one[i]} for i in range(2)}
        ss = {"sq": None}

        def project_sb(p):
            u = Unit()
            qk, old = place(4 + p)
            got = []
            for sub in range(2):
                b = pr.next()
                t = group_cols(u, b, hs2, h_tok, sub)
                t1 = act(A.activation, qk[sub], b.ap, ACT.Copy, scale=(0.125, 1.0)[sub],
                         w=[t, old], s=S("a_q"))
                b.free = [t1]
                got.append(t1)
            u.over(t)
            sbk.qk[p] = (*qk, got)
            push_pair(sbk, p)

        def project_ca(p):
            u = Unit()
            qk, old = place(p)
            got = []
            before = ca.qk[p - 1][2] if p else [None, None]
            for sub in range(2):
                b = pr.next()
                t = group_cols(u, b, hs2, h_tok, sub)
                assert len(before) == 2
                ts = act(A.activation, sq[:, sub, :], b.ap, ACT.Square, w=[t, two_used[sub], ss["sq"]],
                         s=S("a_sqk"))
                t1 = dve(V.tensor_scalar, qk[sub], b.ap, c_gqk[:, sub:sub + 1],
                         (0.125, 1.0)[sub], ALU.mult, ALU.mult, w=[t, ts, old, t_small], s=S("v_q"))
                b.free = [ts, t1]
                got.append((ts, t1))
            u.over(t)
            ca.qk[p] = (*qk, [])

            def scale(sub):
                b = ca.tring.next()
                b.busy = True
                t = pe(T.matmul, b.ap, blk[:, :], sq[:, sub, :], start=True, stop=True,
                       w=[got[sub][0], b.free, t_const], s=S("t_ss"))
                yield
                t1 = act(A.activation, sq[:, sub, :], b.ap, ACT.Ln, scale=1.0 / 64, bias=eps[:, :], w=t,
                         s=S("a_ln"))
                b.freed(t1)
                t1 = act(A.activation, sq[:, sub, :], sq[:, sub, :], ACT.Exp, scale=-0.5, w=t1, s=S("a_ln"))
                yield
                ca.qk[p][2].append(dve(V.tensor_tensor, qk[sub], qk[sub], sq[:, sub, :], ALU.mult,
                                       w=[t1, got[sub][1]], s=S("v_q")))
                ss["sq"] = ca.qk[p][2][-1]

            for sub in range(2):
                queue.insert(min(2 * sub + 2, len(queue)), lambda sub=sub: flush() or begin(scale(sub)))
            push_pair(ca, p)

        for p in range(4):
            project_ca(p)
        mine, bk = other_banks()
        ca.tring, ca.oring = rotating([banks[6]]), rotating([mine])
        group_rows(hs2, h_tok, [0, 128, 256, 384], bk, value_parts(sbk, [128] * 4))
        ca.tring, ca.oring = tring, oring
        st["rate"] = RATE_SB
        for p in range(4):
            project_sb(p)
        push_head(None, None)

        w2 = ExitStack()
        kp = {}

        def attention_over():
            drain()
            st["rate"] = 0
            b2.close()
            kp["over"] = [S("t_pv").now(), S("t_tp").now(), S("a_pt").now(), S("v_pt").now(), at_tok[3]]
            kp["x"], kp["xn"] = sb("x1b", [128, 4, D], where=w2), sb("xnb", [128, 4, D], where=w2)
            for i in range(4):
                t_x1[i] = sp(SY.dma_start, kp["x"][:, i, :], kept[i], w=[kp["over"], t_kept], s=DS(f"d_x{i}"))
            tmp_used.update({0: S("v_tmp").now(), 1: at_tok[3]})

        tmp_used, t_x1 = {}, {}
        res = {}

        def add_gated(j, ch):
            def evac(i, b, t):
                o = kp["x"][:, i, 512 * ch:512 * ch + 512]
                d = tmp[:, i % 2, :]
                t1 = dve(V.tensor_tensor, d, b.ap, gt[:, j, 512 * ch:512 * ch + 512], ALU.mult,
                         w=[t, mod_tok[{0: 2, 1: 5}[j]], tmp_used[i % 2], S("a_sq").now()], s=S("v_tmp"))
                b.free = [t1]
                res[i, ch] = tmp_used[i % 2] = dve(V.tensor_tensor, o, o, d, ALU.add,
                                                   w=[t1, t_x1[i], res.get((i, ch))], s=S("v_tmp"))
            return evac

        normed = {}

        def norm_again(i):
            xi = kp["x"][:, i, :]
            t = square_sum(xi, 420 + i, [res[i, 0], res[i, 1]])
            yield
            r = rstd(t, 420 + i, 1, 1.0 / D)
            yield
            t = dve(V.tensor_scalar, kp["xn"][:, i, :], xi, sm[:, 420 + i:421 + i], None, ALU.mult,
                    w=[r, kp["over"]], s=S("v_xn"))
            normed[i] = (kp["xn"][:, i, :], t)

        def evac_o(ch):
            add = add_gated(0, ch)

            def evac(i, b, t):
                add(i, b, t)
                if ch:
                    tick()
                    chains.append(norm_again(i))
            return evac

        mine, bk = other_banks()
        for a_ in (ca, sbk):
            a_.tring, a_.oring = rotating([banks[6]]), rotating([mine])
        tiles = [0, 128, 256, 384]
        st["rate"] = RATE_WO
        group_rows((ah, al), at_tok, tiles, bk, evac_o(0), (1, 0), mid=attention_over)
        t = group_rows((ah, al), at_tok, tiles, [banks[4], banks[5], banks[6], mine], evac_o(1), (1, 0))
        x1 = kp["x"]
        at_free[0] = t
        h_over = S("t_mm").now()
        while chains:
            tick()
        two_used = [ss["sq"], ss["sq"]]
        h_tok, ahead = transposed([normed[i] for i in range(4)], rotating(banks[0:4]), take_mod(2, h_over))

        r_sb = two
        tmp_used = {0: S("a_sq").now(), 1: S("a_sq").now()}
        pr = rotating(banks[0:4])
        r_used = [None, None]
        a_old = at_free[0]
        s2 = (sgt[:, 0:512], sgt[:, 512:1024])
        s_used = [[ca.used[6], ca.used[7]]] * 2
        t_out = []
        for q in range(4):
            for j in range(4):
                u = Unit()
                start = q == 0 and j == 0
                if start:
                    for k in range(8):
                        ahead(k)
                        for sub in range(2):
                            o = k * 256 + sub * 128
                            t = three(banks[4 + sub].ap, u.h[:, o:o + 128], u.l[:, o:o + 128], hs2[0][:, k, 0:SEQ],
                                      hs2[1][:, k, 0:SEQ], k == 0, k == 7,
                                      w=[h_tok[k], u.t[o // 512], banks[4 + sub].free if k == 0 else None],
                                      s=S("t_mm") if k == 7 else None)
                        u.slot()
                for sub in range(2):
                    n = 2 * j + sub
                    if start:
                        b = banks[4 + sub]
                    else:
                        b = pr.next()
                        t = group_cols(u, b, hs2, h_tok, sub)
                    t1 = act(A.activation, r_sb[:, sub, :], b.ap, ACT.Relu, w=[t, r_used[sub] or two_used[sub]], s=S("a_r"))
                    t2 = dve(V.scalar_tensor_tensor, s2[sub], b.ap, 0.0, r_sb[:, sub, :], ALU.max, ALU.mult,
                             w=[t1, t, s_used[sub]], s=S("v_r2"))
                    r_used[sub] = t2
                    b.free = [t1, t2]
                    s_used[sub] = at_tok[n] = split_sb(ah[:, n, :], al[:, n, :], s2[sub], [t2, a_old])
                u.over(t)
            for ch in range(2):
                bk = banks[4:8] if ch == 0 else banks[0:4]
                evac = add_gated(1, ch)

                def last(i, b, t, evac=evac, ch=ch):
                    evac(i, b, t)
                    t_out.append(act(A.dma_start, out[128 * i:128 * i + 128, 512 * ch:512 * ch + 512],
                                     x1[:, i, 512 * ch:512 * ch + 512], w=res[i, ch], s=DS("d_out")))
                t = group_rows((ah, al), at_tok, [0, 128, 256, 384], bk, last if q == 3 else evac)
            a_old = t
        w2.close()

        block = ctx.enter_context(nc.Block())

        @block.sync
        def _(eng):
            sp.run(eng)
            eng.wait_ge(t_crow[0].sem, t_crow[1])
            for s_, v in t_kept:
                eng.wait_ge(s_.sem, v)

        @block.scalar
        def _(eng):
            act.run(eng)
            eng.wait_ge(t_out[-1][0].sem, t_out[-1][1])

        @block.vector
        def _(eng):
            dve.run(eng)

        @block.gpsimd
        def _(eng):
            pool.run(eng)

        @block.tensor
        def _(eng):
            pe.run(eng)


def kernel(x, meta_tokens, norm_g, w_in, b_forget, pool_w, pool_scale, w_up_pool, w_up_attn, w_out, final_norm_g,
           c_2, g_norm1_2, w_in_2, g_q_2, g_k_2, rel_bias_2, w_o_2, g_norm2_2, w1_2, w2_2, w_ada_2, b_ada_2):
    import numpy as np
    import concourse.bacc as bacc
    from concourse.bass_utils import run_bass_kernel_spmd

    a = {n: np.asarray(v)[0] for n, v in dict(w_in=w_in, w_out=w_out, w_in_2=w_in_2, w_o_2=w_o_2, w1_2=w1_2,
                                              w2_2=w2_2, w_ada_2=w_ada_2, up=w_up_pool, ua=w_up_attn).items()}

    def columns(v):
        return np.ascontiguousarray(np.asarray(v).reshape(-1, 128).T)

    def packed(unit):
        kind, name, p, q = unit
        if kind == "cols":
            w = a[name]
            both = np.concatenate([w[:, p:p + 128], w[:, q:q + 128]], 1)
            return both.reshape(8, 128, 256).transpose(1, 0, 2).reshape(128, UNIT)
        if kind == "rows":
            return a[name][512 * p:512 * p + 512, q:q + 512].reshape(4, 128, 512).transpose(1, 0, 2).reshape(128, UNIT)
        if kind == "ada":
            return a[name][128 * p:128 * p + 128, UNIT * q:UNIT * q + UNIT]
        tiles = [a[s][:, 128 * d:128 * d + 128].reshape(4, 128, 128).transpose(1, 0, 2).reshape(128, 512)
                 for d in (2 * p, 2 * p + 1) for s in ("up", "ua")]
        return np.concatenate(tiles, 1)

    f = np.tile(a["w_in"][:, C_F:C_F + 8], (1, 16)).reshape(8, 128, 128).transpose(1, 0, 2)
    far = np.clip(384 + np.arange(128)[:, None] - np.arange(512)[None, :], -128, 128) + 128
    rel = np.asarray(rel_bias_2)[0][:, far]
    arrays = {
        "x": np.asarray(x)[0],
        "meta": np.asarray(meta_tokens),
        "wall": np.stack([packed(u) for u in plan()]),
        "wf": f,
        "poolw": np.asarray(pool_w)[0].transpose(1, 0, 2).reshape(128, 512),
        "params": np.concatenate([
            columns(np.asarray(norm_g)[0]), columns(np.asarray(pool_scale)[0]), columns(np.asarray(g_norm1_2)[0]),
            columns(np.asarray(g_norm2_2)[0]), columns(np.asarray(c_2)[0]),
            np.stack([np.tile(np.asarray(g_q_2)[0], 2), np.tile(np.asarray(g_k_2)[0], 2)], 1),
            np.tile(np.asarray(b_forget)[0], 16).reshape(128, 1)], 1),
        "fng": np.asarray(final_norm_g).reshape(1, D),
        "bada": np.asarray(b_ada_2)[0].reshape(3, UNIT),
        "rel": rel,
    }
    arrays = {n: np.ascontiguousarray(v) for n, v in arrays.items()}
    nc = bacc.Bacc("TRN2", target_bir_lowering=False, num_devices=1, dynamic_dma_scratch_size=1024)
    args = [nc.dram_tensor("in_" + n, v.shape, mybir.dt.from_np(v.dtype), kind="ExternalInput").ap()
            for n, v in arrays.items()]
    out = nc.dram_tensor("out", (SEQ, D), F32, kind="ExternalOutput").ap()
    program(nc, *args, out)
    r = run_bass_kernel_spmd(nc, [{"in_" + n: v for n, v in arrays.items()}], core_ids=[0])
    return r.results[0]["out"].reshape(1, SEQ, D)
```
